# Optimizing a Trainium2 kernel written in Bass

```python
import math
import jax
import jax.numpy as jnp
from jax import lax
import numpy as np

D_MODEL = 1024
BATCH = 1
SEQ = 256
DEPTH = 2

GRID_W = 64
CTX_LEN = 256
HEAD_DIM = 64
N_MOD = 6
NORM_EPS = 1e-6
ROPE_BASE = 10000.0
BLOCK = 128

HY_GROUPS = 4
HY_WIDTH = HY_GROUPS * HEAD_DIM
HY_ORDER = 2
HY_BANDS = 16
HY_EMB_DIM = 1 + 2 * HY_BANDS
HY_FILTER_WIDTH = 64
HY_SHORT_CONV = 3
HY_DECAY_MIN = 3.07
HY_DECAY_MAX = 15.35

WA_Q_HEADS = 8
WA_KV_HEADS = 2
WA_GROUP = WA_Q_HEADS // WA_KV_HEADS
WINDOW = 128

DA_HEADS = 4
DA_QK_DIM = 32
DA_V_DIM = 2 * DA_QK_DIM
DA_LAMBDA_BASE = 0.8
DA_LAMBDA_AMP = 0.6
DA_LAMBDA_RATE = 0.3

HY_COLS = (HY_ORDER + 1) * HY_WIDTH
WA_Q_COLS = WA_Q_HEADS * HEAD_DIM
WA_KV_COLS = WA_KV_HEADS * HEAD_DIM
WA_COLS = WA_Q_COLS + 2 * WA_KV_COLS
DA_QK_COLS = DA_HEADS * 2 * DA_QK_DIM
DA_COLS = 2 * DA_QK_COLS + DA_HEADS * DA_V_DIM
IN_COLS = HY_COLS + WA_COLS + DA_COLS
MIX_WIDTH = HY_WIDTH + WA_Q_COLS + DA_HEADS * DA_V_DIM

PEER_HEADS = 8
N_KEYS = 128
N_EXPERTS = N_KEYS * N_KEYS
PEER_TOPK = 16
PEER_QDIM = 256
TOKEN_CHUNK = 128

kernel_name = 'hybrid_hyena_swa_diffattn_peer_dit'

def rmsnorm(x, g):
    xf = x.astype(jnp.float32)
    y = xf * lax.rsqrt(jnp.mean(xf * xf, axis=-1, keepdims=True) + NORM_EPS)
    return (y * g.astype(jnp.float32)).astype(x.dtype)

def modulate(h, shift, scale):
    return h * (1.0 + scale) + shift

def axial_rope_tables(n_tokens, dim):
    n_rows = n_tokens // GRID_W
    row = jnp.broadcast_to(jnp.arange(n_rows)[:, None], (n_rows, GRID_W)).reshape(-1).astype(jnp.float32)
    col = jnp.broadcast_to(jnp.arange(GRID_W)[None, :], (n_rows, GRID_W)).reshape(-1).astype(jnp.float32)
    axis_dim = dim // 2
    inv_freq = ROPE_BASE ** (-jnp.arange(0, axis_dim, 2, dtype=jnp.float32) / axis_dim)
    ang_r = row[:, None] * inv_freq
    ang_c = col[:, None] * inv_freq
    return (jnp.cos(ang_r), jnp.sin(ang_r), jnp.cos(ang_c), jnp.sin(ang_c))

def _rotate_half(x, cos, sin):
    m = x.shape[-1] // 2
    x1, x2 = x[..., :m], x[..., m:]
    cos = cos[None, :, None, :]
    sin = sin[None, :, None, :]
    return jnp.concatenate([x1 * cos - x2 * sin, x2 * cos + x1 * sin], axis=-1)

def apply_axial_rope(x, tables):
    cr, sr, cc, sc = tables
    half = x.shape[-1] // 2
    xf = x.astype(jnp.float32)
    out = jnp.concatenate([_rotate_half(xf[..., :half], cr, sr), _rotate_half(xf[..., half:], cc, sc)], axis=-1)
    return out.astype(x.dtype)

def short_conv(u, w, b):
    n = u.shape[1]
    pad = HY_SHORT_CONV // 2
    up = jnp.pad(u, ((0, 0), (pad, pad), (0, 0)))
    out = b
    for j in range(HY_SHORT_CONV):
        out = out + up[:, j:j + n] * w[j]
    return out

def hyena_filters(n, lp):
    f32 = jnp.float32
    t = jnp.linspace(0.0, 1.0, n, dtype=f32)[:, None]
    bands = jnp.linspace(1e-4, HY_BANDS - 1, HY_BANDS, dtype=f32)
    phase = (2.0 * math.pi / n) * jnp.arange(n, dtype=f32)[:, None] * bands
    feat = jnp.concatenate([t, jnp.cos(phase), -jnp.sin(phase)], axis=-1)
    freq = lp['hy_freq'].astype(f32)
    z = jnp.sin(freq * (feat @ lp['hy_w1'].astype(f32) + lp['hy_b1'].astype(f32)))
    z = jnp.sin(freq * (z @ lp['hy_w2'].astype(f32) + lp['hy_b2'].astype(f32)))
    h = (z @ lp['hy_w3'].astype(f32)).reshape(n, HY_ORDER, 2, HY_WIDTH)
    window = jnp.exp(-t[:, :, None, None] * jnp.abs(lp['hy_decay'].astype(f32)))
    return h * window

def two_sided_spectrum(h):
    fwd = h[:, :, 0]
    bwd = h[:0:-1, :, 1]
    full = jnp.concatenate([fwd, jnp.zeros_like(fwd[:1]), bwd], axis=0)
    return jnp.fft.rfft(full, axis=0)

def hyena_mixer(u, lp):
    n = u.shape[1]
    parts = jnp.split(short_conv(u, lp['hy_conv_w'], lp['hy_conv_b']).astype(jnp.float32), HY_ORDER + 1, axis=-1)
    z = parts[-1]
    spec = two_sided_spectrum(hyena_filters(n, lp))
    bias = lp['hy_bias'].astype(jnp.float32)
    for o in range(HY_ORDER):
        zf = jnp.fft.rfft(z, n=2 * n, axis=1)
        conv = jnp.fft.irfft(zf * spec[None, :, o], n=2 * n, axis=1)[:, :n]
        z = parts[o] * (conv + bias[o] * z)
    return z.astype(u.dtype)

def window_gqa_latent(q, k, v, kc, vc, sink):
    B, S = q.shape[:2]
    nb = S // BLOCK
    scale = HEAD_DIM ** -0.5
    qb = q.reshape(B, nb, BLOCK, WA_KV_HEADS, WA_GROUP, HEAD_DIM)

    def band(t):
        tp = jnp.pad(t, ((0, 0), (BLOCK, BLOCK), (0, 0), (0, 0))).reshape(B, nb + 2, BLOCK, WA_KV_HEADS, HEAD_DIM)
        return jnp.concatenate([tp[:, :-2], tp[:, 1:-1], tp[:, 2:]], axis=2)

    kw, vw = band(k), band(v)
    qpos = jnp.arange(nb)[:, None] * BLOCK + jnp.arange(BLOCK)[None, :]
    kpos = jnp.arange(nb)[:, None] * BLOCK - BLOCK + jnp.arange(3 * BLOCK)[None, :]
    valid = ((jnp.abs(qpos[:, :, None] - kpos[:, None, :]) <= WINDOW)
             & (kpos[:, None, :] >= 0) & (kpos[:, None, :] < S))
    s_loc = jnp.einsum('bnqhgd,bnkhd->bnhgqk', qb, kw).astype(jnp.float32) * scale
    s_loc = jnp.where(valid[None, :, None, None], s_loc, -jnp.inf)
    s_ctx = jnp.einsum('bnqhgd,bchd->bnhgqc', qb, kc).astype(jnp.float32) * scale
    s_sink = jnp.broadcast_to(sink.astype(jnp.float32).reshape(WA_KV_HEADS, WA_GROUP)[None, None, :, :, None, None],
                              s_ctx.shape[:-1] + (1,))
    p = jax.nn.softmax(jnp.concatenate([s_loc, s_ctx, s_sink], axis=-1), axis=-1)
    n_loc = 3 * BLOCK
    n_ctx = kc.shape[1]
    out = (jnp.einsum('bnhgqk,bnkhd->bnqhgd', p[..., :n_loc].astype(v.dtype), vw)
           + jnp.einsum('bnhgqc,bchd->bnqhgd', p[..., n_loc:n_loc + n_ctx].astype(v.dtype), vc))
    return out.reshape(B, S, WA_Q_COLS)

def gqa_context(qc, kc, vc, sink):
    B, C = qc.shape[:2]
    q = qc.reshape(B, C, WA_KV_HEADS, WA_GROUP, HEAD_DIM)
    s = jnp.einsum('bqhgd,bkhd->bhgqk', q, kc).astype(jnp.float32) * HEAD_DIM ** -0.5
    s_sink = jnp.broadcast_to(sink.astype(jnp.float32).reshape(WA_KV_HEADS, WA_GROUP)[None, :, :, None, None],
                              s.shape[:-1] + (1,))
    p = jax.nn.softmax(jnp.concatenate([s, s_sink], axis=-1), axis=-1)[..., :C]
    return jnp.einsum('bhgqk,bkhd->bqhgd', p.astype(vc.dtype), vc).reshape(B, C, WA_Q_COLS)

def diff_lambda(lp, lam_init):
    f32 = jnp.float32
    return (jnp.exp(jnp.sum(lp['da_lq1'].astype(f32) * lp['da_lk1'].astype(f32)))
            - jnp.exp(jnp.sum(lp['da_lq2'].astype(f32) * lp['da_lk2'].astype(f32))) + lam_init)

def diff_attend(qb, k, v, lam):
    s = jnp.einsum('bqhmd,bkhmd->bhmqk', qb, k).astype(jnp.float32) * DA_QK_DIM ** -0.5
    p = jax.nn.softmax(s, axis=-1)
    a = p[:, :, 0] - lam * p[:, :, 1]
    return jnp.einsum('bhqk,bkhd->bqhd', a, v.astype(jnp.float32))

def diff_latent(q, k, v, kc, vc, lam):
    B, S = q.shape[:2]
    nb = S // BLOCK
    k_all = jnp.concatenate([k, kc], axis=1)
    v_all = jnp.concatenate([v, vc], axis=1)
    qblocks = jnp.moveaxis(q.reshape(B, nb, BLOCK, DA_HEADS, 2, DA_QK_DIM), 1, 0)
    out = lax.map(lambda qb: diff_attend(qb, k_all, v_all, lam), qblocks)
    return jnp.moveaxis(out, 0, 1).reshape(B, S, DA_HEADS, DA_V_DIM)

def diff_out(o, g, lam_init):
    B, L = o.shape[:2]
    return (rmsnorm(o, g) * (1.0 - lam_init)).reshape(B, L, DA_HEADS * DA_V_DIM)

def merge_heads(y_hy, y_wa, y_da, w_out, dtype):
    y = jnp.concatenate([y_hy.astype(dtype), y_wa.astype(dtype), y_da.astype(dtype)], axis=-1)
    return y @ w_out

def token_mixer(h, hc, lp, rope_wa, rope_da, lam_init, need_ctx_out):
    B, S, _ = h.shape
    C = hc.shape[1]
    cuts = (HY_COLS, HY_COLS + WA_COLS)
    hy, wa, da = jnp.split(h @ lp['w_in'], cuts, axis=-1)
    pc = hc @ lp['w_in']
    wa_c = pc[..., HY_COLS:HY_COLS + WA_COLS]
    da_c = pc[..., HY_COLS + WA_COLS:]
    y_hy = hyena_mixer(hy, lp)
    q, k, v = jnp.split(wa, (WA_Q_COLS, WA_Q_COLS + WA_KV_COLS), axis=-1)
    q = apply_axial_rope(q.reshape(B, S, WA_Q_HEADS, HEAD_DIM), rope_wa)
    k = apply_axial_rope(k.reshape(B, S, WA_KV_HEADS, HEAD_DIM), rope_wa)
    v = v.reshape(B, S, WA_KV_HEADS, HEAD_DIM)
    kc = wa_c[..., WA_Q_COLS:WA_Q_COLS + WA_KV_COLS].reshape(B, C, WA_KV_HEADS, HEAD_DIM)
    vc = wa_c[..., WA_Q_COLS + WA_KV_COLS:].reshape(B, C, WA_KV_HEADS, HEAD_DIM)
    y_wa = window_gqa_latent(q, k, v, kc, vc, lp['wa_sink'])
    lam = diff_lambda(lp, lam_init)
    q2, k2, v2 = jnp.split(da, (DA_QK_COLS, 2 * DA_QK_COLS), axis=-1)
    q2 = apply_axial_rope(q2.reshape(B, S, DA_HEADS * 2, DA_QK_DIM), rope_da).reshape(B, S, DA_HEADS, 2, DA_QK_DIM)
    k2 = apply_axial_rope(k2.reshape(B, S, DA_HEADS * 2, DA_QK_DIM), rope_da).reshape(B, S, DA_HEADS, 2, DA_QK_DIM)
    v2 = v2.reshape(B, S, DA_HEADS, DA_V_DIM)
    k2c = da_c[..., DA_QK_COLS:2 * DA_QK_COLS].reshape(B, C, DA_HEADS, 2, DA_QK_DIM)
    v2c = da_c[..., 2 * DA_QK_COLS:].reshape(B, C, DA_HEADS, DA_V_DIM)
    y_da = diff_out(diff_latent(q2, k2, v2, k2c, v2c, lam), lp['da_norm_g'], lam_init)
    y = merge_heads(y_hy, y_wa, y_da, lp['w_out'], h.dtype)
    if not need_ctx_out:
        return y, None
    yc_hy = hyena_mixer(pc[..., :HY_COLS], lp)
    qc = wa_c[..., :WA_Q_COLS].reshape(B, C, WA_Q_HEADS, HEAD_DIM)
    yc_wa = gqa_context(qc, kc, vc, lp['wa_sink'])
    q2c = da_c[..., :DA_QK_COLS].reshape(B, C, DA_HEADS, 2, DA_QK_DIM)
    yc_da = diff_out(diff_attend(q2c, k2c, v2c, lam), lp['da_norm_g'], lam_init)
    yc = merge_heads(yc_hy, yc_wa, yc_da, lp['w_out'], hc.dtype)
    return y, yc

def peer_ffn(h, wq, keys, u, v):
    T, D = h.shape
    half = PEER_QDIM // 2
    chunks = h.reshape(T // TOKEN_CHUNK, TOKEN_CHUNK, D)

    def one_chunk(xc):
        q = (xc @ wq).reshape(TOKEN_CHUNK, PEER_HEADS, 2, half)
        s = jnp.einsum('thpd,hpkd->thpk', q, keys).astype(jnp.float32)
        s_top, i_top = lax.top_k(s, PEER_TOPK)
        cand_s = (s_top[:, :, 0, :, None] + s_top[:, :, 1, None, :]).reshape(TOKEN_CHUNK, PEER_HEADS, PEER_TOPK * PEER_TOPK)
        cand_i = (i_top[:, :, 0, :, None] * N_KEYS + i_top[:, :, 1, None, :]).reshape(TOKEN_CHUNK, PEER_HEADS, PEER_TOPK * PEER_TOPK)
        best_s, best_j = lax.top_k(cand_s, PEER_TOPK)
        idx = jnp.take_along_axis(cand_i, best_j, axis=-1)
        gate = jax.nn.softmax(best_s, axis=-1)
        act = jax.nn.gelu(jnp.einsum('thkd,td->thk', u[idx], xc).astype(jnp.float32), approximate=False)
        return jnp.einsum('thk,thkd->td', (gate * act).astype(v.dtype), v[idx])

    return lax.map(one_chunk, chunks).reshape(T, D)

def setup_inputs(seed: int = 0) -> dict:
    key = jax.random.key(seed)
    ks = jax.random.split(key, 32)
    f32 = jnp.float32
    D = D_MODEL
    L = DEPTH
    FW = HY_FILTER_WIDTH

    def nrm(k, shape, s):
        return jax.random.normal(k, shape, f32) * s

    decay0 = jnp.broadcast_to(jnp.linspace(HY_DECAY_MIN, HY_DECAY_MAX, HY_WIDTH, dtype=f32), (L, HY_ORDER, 2, HY_WIDTH))
    return {
        'x': nrm(ks[0], (BATCH, SEQ, D), 1.0),
        'c': nrm(ks[1], (BATCH, D), 1.0),
        'ctx': nrm(ks[2], (BATCH, CTX_LEN, D), 1.0),
        'c_ctx': nrm(ks[3], (D,), 1.0),
        'w_mod': nrm(ks[4], (L, D, N_MOD * D), D ** -0.5),
        'b_mod': nrm(ks[5], (L, N_MOD * D), 0.02),
        'norm1_g': 1.0 + nrm(ks[6], (L, D), 0.02),
        'w_in': nrm(ks[7], (L, D, IN_COLS), D ** -0.5),
        'hy_conv_w': nrm(ks[8], (L, HY_SHORT_CONV, HY_COLS), HY_SHORT_CONV ** -0.5),
        'hy_conv_b': nrm(ks[9], (L, HY_COLS), 0.02),
        'hy_w1': nrm(ks[10], (L, HY_EMB_DIM, FW), HY_EMB_DIM ** -0.5),
        'hy_b1': nrm(ks[11], (L, FW), 0.02),
        'hy_freq': 1.0 + nrm(ks[12], (L, FW), 0.02),
        'hy_w2': nrm(ks[13], (L, FW, FW), FW ** -0.5),
        'hy_b2': nrm(ks[14], (L, FW), 0.02),
        'hy_w3': nrm(ks[15], (L, FW, HY_ORDER * 2 * HY_WIDTH), 0.05 * FW ** -0.5),
        'hy_decay': decay0 * (1.0 + nrm(ks[16], (L, HY_ORDER, 2, HY_WIDTH), 0.05)),
        'hy_bias': nrm(ks[17], (L, HY_ORDER, HY_WIDTH), 1.0),
        'wa_sink': nrm(ks[18], (L, WA_Q_HEADS), 1.0),
        'da_lq1': nrm(ks[19], (L, DA_QK_DIM), 0.1),
        'da_lk1': nrm(ks[20], (L, DA_QK_DIM), 0.1),
        'da_lq2': nrm(ks[21], (L, DA_QK_DIM), 0.1),
        'da_lk2': nrm(ks[22], (L, DA_QK_DIM), 0.1),
        'da_norm_g': 1.0 + nrm(ks[23], (L, DA_V_DIM), 0.02),
        'w_out': nrm(ks[24], (L, MIX_WIDTH, D), MIX_WIDTH ** -0.5),
        'norm2_g': 1.0 + nrm(ks[25], (L, D), 0.02),
        'peer_wq': nrm(ks[26], (L, D, PEER_HEADS * PEER_QDIM), D ** -0.5),
        'peer_keys': nrm(ks[27], (L, PEER_HEADS, 2, N_KEYS, PEER_QDIM // 2), (PEER_QDIM // 2) ** -0.5),
        'peer_u': nrm(ks[28], (L, N_EXPERTS, D), D ** -0.5),
        'peer_v': nrm(ks[29], (L, N_EXPERTS, D), 0.5),
        'final_g': 1.0 + nrm(ks[30], (D,), 0.02),
    }

def reference(x, c, ctx, c_ctx, w_mod, b_mod, norm1_g, w_in, hy_conv_w, hy_conv_b, hy_w1, hy_b1, hy_freq,
              hy_w2, hy_b2, hy_w3, hy_decay, hy_bias, wa_sink, da_lq1, da_lk1, da_lq2, da_lk2, da_norm_g,
              w_out, norm2_g, peer_wq, peer_keys, peer_u, peer_v, final_g):
    batch, n_lat, d = x.shape
    n_ctx = ctx.shape[1]
    rope_wa = axial_rope_tables(n_lat, HEAD_DIM)
    rope_da = axial_rope_tables(n_lat, DA_QK_DIM)
    c_act = jax.nn.silu(c)
    cc_act = jax.nn.silu(c_ctx)
    xc = ctx
    for li in range(DEPTH):
        need_ctx = li < DEPTH - 1
        lam_init = DA_LAMBDA_BASE - DA_LAMBDA_AMP * math.exp(-DA_LAMBDA_RATE * li)
        lp = {
            'w_in': w_in[li], 'w_out': w_out[li],
            'hy_conv_w': hy_conv_w[li], 'hy_conv_b': hy_conv_b[li],
            'hy_w1': hy_w1[li], 'hy_b1': hy_b1[li], 'hy_freq': hy_freq[li],
            'hy_w2': hy_w2[li], 'hy_b2': hy_b2[li], 'hy_w3': hy_w3[li],
            'hy_decay': hy_decay[li], 'hy_bias': hy_bias[li],
            'wa_sink': wa_sink[li],
            'da_lq1': da_lq1[li], 'da_lk1': da_lk1[li], 'da_lq2': da_lq2[li], 'da_lk2': da_lk2[li],
            'da_norm_g': da_norm_g[li],
        }
        mod = jnp.split((c_act @ w_mod[li] + b_mod[li])[:, None, :], N_MOD, axis=-1)
        modc = jnp.split((cc_act @ w_mod[li] + b_mod[li])[None, None, :], N_MOD, axis=-1)
        h = modulate(rmsnorm(x, norm1_g[li]), mod[0], mod[1])
        hc = modulate(rmsnorm(xc, norm1_g[li]), modc[0], modc[1])
        y, yc = token_mixer(h, hc, lp, rope_wa, rope_da, lam_init, need_ctx)
        x = x + mod[2] * y
        h2 = modulate(rmsnorm(x, norm2_g[li]), mod[3], mod[4])
        if need_ctx:
            xc = xc + modc[2] * yc
            h2c = modulate(rmsnorm(xc, norm2_g[li]), modc[3], modc[4])
            tok = jnp.concatenate([h2.reshape(-1, d), h2c.reshape(-1, d)], axis=0)
            out = peer_ffn(tok, peer_wq[li], peer_keys[li], peer_u[li], peer_v[li])
            x = x + mod[5] * out[:batch * n_lat].reshape(batch, n_lat, d)
            xc = xc + modc[5] * out[batch * n_lat:].reshape(batch, n_ctx, d)
        else:
            out = peer_ffn(h2.reshape(-1, d), peer_wq[li], peer_keys[li], peer_u[li], peer_v[li])
            x = x + mod[5] * out.reshape(batch, n_lat, d)
    return rmsnorm(x, final_g)


_drawn_inputs = setup_inputs


def setup_inputs(seed=0):
    import zlib

    import numpy as np

    out = dict(_drawn_inputs(seed))
    spreads = {}
    factors = {'hy_freq': 3.711, 'wa_sink': 7.821, 'da_lq1': 3.739, 'da_lk1': 3.735, 'final_g': 2.743}
    for name, (base, spread) in spreads.items():
        noise = np.random.default_rng([zlib.crc32(name.encode()), seed]).standard_normal(out[name].shape)
        drawn = base * np.exp(spread * noise) if base else spread * noise
        out[name] = jnp.asarray(drawn.astype(out[name].dtype))
    for name, factor in factors.items():
        out[name] = (out[name] * factor).astype(out[name].dtype)
    return out
```

```python
import math
from contextlib import ExitStack

import concourse.bass as bass
import numpy as np
from concourse import mybir

F32 = mybir.dt.float32
U32 = mybir.dt.uint32
ALU = mybir.AluOpType
ACT = mybir.ActivationFunctionType
AX = mybir.AxisListType.X

P = 128
D = 1024
KD = D // P
SEQ = 256
LAYERS = 2
GRID_W = 64
EPS = 1e-6
HYW = 256
HY_COLS = 3 * HYW
FW = 64
EMB = 33
IN_COLS = 2304
WA0 = HY_COLS
DA0 = 1536
WA_HEADS, WA_KV = 8, 2
WA_SCALE = 64 ** -0.5
DA_HEADS = 4
DA_SCALE = 32 ** -0.5
HEADS = 8
TOPK = 16
NKEYS = 128
NEXP = NKEYS * NKEYS
NMOD_CHUNKS = 48
LOW = -3.0e38
BANKS = 6
SLOTS = 4
SLOT_W = 3072
U_SLOTS, V_SLOTS, G_SLOTS = 8, 4, 4
C1 = 6.28125
C2 = 2.0 * math.pi - C1
ROUND = 12582912.0
PI_IN = 3.1415925


def lam_init_of(layer):
    return 0.8 - 0.6 * math.exp(-0.3 * layer)


def q_tiles(layer):
    return 4 if layer < LAYERS - 1 else 2


def streams(layer):
    return q_tiles(layer) // 2


LOADS = []
for _l in range(LAYERS):
    LOADS += [("mod", _l, n) for n in range(16)]
    LOADS += [("in", _l, n) for n in range(6)]
    LOADS += [("out", _l, n) for n in range(4)]
    LOADS += [("q", _l, n) for n in range(8)]
LOAD_AT = {key: n for n, key in enumerate(LOADS)}


def proj_units(layer):
    return [(c, t) for c in range(6) for t in range(4 if (layer < LAYERS - 1 or c >= 3) else 2)]


def attention_maps(layer):
    out = []
    for t in range(q_tiles(layer)):
        out += [("wa", t, h, 0) for h in range(WA_HEADS)]
        out += [("da", t, h, m) for h in range(DA_HEADS) for m in range(2)]
    return out


def stat_column(kind, t, h, m):
    return t * WA_HEADS + h if kind == "wa" else 32 + (t * DA_HEADS + h) * 2 + m


def has_pv(unit):
    return unit[0] == "wa" or unit[3] == 1


GROUPS = []


def _group(key, engine):
    GROUPS.append((key, engine))


def _plan():
    flip = ("dve", "act")
    for l in range(LAYERS):
        _group(("flt1", l), "dve")
        _group(("flt2", l), "dve")
        for tt in range(2):
            for o in range(2):
                _group(("flt3", l, tt, o), "dve")
        for n in range(5):
            _group(("spec", l, n), "act")
        for n in range(16):
            _group(("mod", l, n), "dve")
        for kk in range(KD):
            _group(("hT", l, kk), flip[kk % 2])
        for c, t in proj_units(l):
            _group(("pj", l, c, t), flip[t % 2])
        for b in range(9):
            _group(("tr", l, b), "act")
        for o in range(2):
            for m in range(2):
                _group(("re", l, o, m), "dve")
                _group(("im", l, o, m), "dve")
            for tt in range(2):
                _group(("inv", l, o, tt), "dve")
        maps = attention_maps(l)

        def score(n):
            _group(("s", l, n), "dve" if maps[n][0] == "wa" and maps[n][1] < 2 else "act")
        score(0)
        score(1)
        for n, unit in enumerate(maps):
            if n + 2 < len(maps):
                score(n + 2)
            if has_pv(unit):
                _group(("pt", l, n), "act" if n % 4 == 1 else "dve")
        for v in range(3):
            for s in range(streams(l)):
                for half in range(2):
                    _group(("bc", l, v, s, half), flip[half])
        for kk in range(KD):
            _group(("yT", l, kk), flip[kk % 2])
        for n in range(4):
            for t in range(q_tiles(l)):
                _group(("wo", l, n, t), "dve")
        for kk in range(KD):
            _group(("h2T", l, kk), flip[kk % 2])
        for hp in range(2 * HEADS):
            _group(("q", l, hp), "act")
            _group(("sc", l, hp), "dve")
        for s in range(streams(l)):
            for half in range(2):
                _group(("bc5", l, s, half), flip[half])


_plan()
GROUP_AT = {key: n for n, (key, _) in enumerate(GROUPS)}
FREED_COUNT = []
_seen = {"dve": 0, "act": 0}
for _key, _engine in GROUPS:
    _seen[_engine] += 1
    FREED_COUNT.append(_seen[_engine])

LAST_USE = {}
for _l in range(LAYERS):
    for _n in range(16):
        LAST_USE["mod", _l, _n] = ("mod", _l, _n)
    for _n in range(6):
        LAST_USE["in", _l, _n] = ("pj", _l, _n, max(t for c, t in proj_units(_l) if c == _n))
    for _n in range(4):
        LAST_USE["out", _l, _n] = ("wo", _l, _n, q_tiles(_l) - 1)
    for _n in range(8):
        LAST_USE["q", _l, _n] = ("q", _l, 2 * _n + 1)

HEADS_BEFORE = [sum(HEADS * q_tiles(k) for k in range(l)) for l in range(LAYERS + 1)]


def build(nc, A, out):
    ctx = ExitStack()
    with ctx:
        def sb(name, shape, dt=F32):
            return ctx.enter_context(nc.sbuf_tensor("t_" + name, shape, dt))

        def sem(name):
            return ctx.enter_context(nc.semaphore(name))

        x_res = sb("x_res", [P, 4, D])
        area_h = sb("area_h", [P, 4096])
        area_p = sb("area_p", [P, 4 * IN_COLS])
        area_a = sb("area_a", [P, 4608])
        area_y = sb("area_y", [P, 4, D])
        ring = sb("ring", [P, SLOTS * SLOT_W])
        area_b = sb("area_b", [P, 6144])

        hT = area_h[:, :].rearrange("p (k t) -> p k t", k=KD)
        yre = area_h[:, 0:1024].rearrange("p (m n) -> p m n", m=2)
        yim = area_h[:, 1024:2048].rearrange("p (m n) -> p m n", m=2)
        z_buf = area_h[:, 2048:3072].rearrange("p (t s c) -> p t s c", t=2, s=2)
        hy_tmp = area_h[:, 3072:3584]
        hy_bias = area_h[:, 3584:4096].rearrange("p (o c) -> p o c", o=2)
        proj = area_p[:, :].rearrange("p (t c) -> p t c", t=4)
        junk = area_p[:, 0:D]
        scores = area_p[:, 0:4 * 2048]
        head_sc = area_p[:, 8192:8704].rearrange("p (b a k) -> p b a k", b=2, a=2)
        f_sum = area_a[:, 0:1024].rearrange("p (t n) -> p t n", t=2)
        f_dif = area_a[:, 1024:2048].rearrange("p (t n) -> p t n", t=2)
        f_win = area_a[:, 2048:3072]
        f_dec = area_a[:, 3072:4096]
        f_hw = area_a[:, 4096:4608]
        qkT = area_a[:, :].rearrange("p (b t) -> p b t", b=9)
        res_tmp = area_a[:, 0:256]
        qT = area_a[:, 0:1024].rearrange("p (b t) -> p b t", b=2)
        o_acc = area_a[:, 0:4096].rearrange("p (t n) -> p t n", t=4)
        diag = area_a[:, 4096:4608].rearrange("p (g n) -> p g n", g=G_SLOTS)
        w3_sb = area_y[0:FW, 0, :]
        f_arg = area_y[0:FW, 1, 0:256]
        f_rnd = area_y[0:FW, 1, 256:512]
        f_z1 = area_y[0:FW, 1, 512:768]
        f_z2 = area_y[0:FW, 1, 768:1024]
        conv_w = area_y[:, 0:3, :].rearrange("p a (b c) -> p (a b c)", b=1).rearrange("p (j c) -> p j c", j=4)
        u_prev = area_b[:, 0:3072].rearrange("p (t c) -> p t c", t=4)
        u_next = area_b[:, 3072:6144].rearrange("p (t c) -> p t c", t=4)
        p_buf = area_b[:, 0:2048].rearrange("p (n k) -> p n k", n=4)
        pT_buf = area_b[:, 2048:3072].rearrange("p (n k) -> p n k", n=2)
        rope_1 = area_b[:, 3072:3712]
        rope_2 = area_b[:, 3712:4352]
        da_sq = area_b[:, 4352:5376].rearrange("p (t c) -> p t c", t=4)
        gate_bc = area_b[:, 0:2048].rearrange("p (s n) -> p s n", s=2)
        a2_bc = area_b[:, 2048:4096].rearrange("p (s n) -> p s n", s=2)
        b2_bc = area_b[:, 4096:6144].rearrange("p (s n) -> p s n", s=2)
        keysT = area_b[:, 2048:4096].rearrange("p (h k) -> p h k", h=16)
        dot_junk = area_b[:, 4096:5120]
        cand = area_b[:, 5120:5376]
        cand2 = area_b[:, 5376:5632]
        onehot = area_b[:, 5632:5888]
        sc_left = area_b[:, 5888:6144].rearrange("p (a k) -> p a k", a=2)
        final_g = area_b[:, 2048:3072]

        y_flat = area_y[:, :, :].rearrange("p t n -> p (t n)")

        def wslot(key):
            s = LOAD_AT[key] % SLOTS
            return ring[:, s * SLOT_W:(s + 1) * SLOT_W]

        u_rows = [ring[:, n * D:(n + 1) * D] for n in range(U_SLOTS)]
        v_rows = [ring[:, (U_SLOTS + n) * D:(U_SLOTS + n + 1) * D] for n in range(V_SLOTS)]

        ident = sb("ident", [P, P])
        dft_c = sb("dft_c", [P, 2, 256])
        dft_s = sb("dft_s", [P, 2, 256])
        dft_i = sb("dft_i", [P, 2, 256])
        dft_cn = sb("dft_cn", [P, 2, P])
        dft_s0 = sb("dft_s0", [P, 2, P])
        cols = sb("cols", [P, 6])
        feat = sb("feat", [EMB, 256])
        rope = sb("rope", [P, 2, 192])
        mask = sb("mask", [P, 2, 512])
        iota16 = sb("iota16", [P, TOPK])
        c_raw = sb("c_raw", [P, KD * 2])
        c_tmp = sb("c_tmp", [P, KD * 2])
        c_act = sb("c_act", [P, KD, 2])
        bmod = sb("bmod", [P, LAYERS, NMOD_CHUNKS])
        g12 = sb("g12", [P, LAYERS, 2, KD])
        sinks = sb("sinks", [P, LAYERS, WA_HEADS])
        nsinks = sb("nsinks", [P, LAYERS, WA_HEADS])
        lam_v = sb("lam_v", [P, 4, LAYERS * 32])
        lam_p = sb("lam_p", [P, 2, LAYERS * 32])
        lam_s = sb("lam_s", [P, 2, LAYERS])
        lam_n = sb("lam_n", [P, LAYERS])
        dag = sb("dag", [P, LAYERS, 64])
        fcol = sb("fcol", [FW, LAYERS, 3])
        w1_sb = sb("w1_sb", [EMB, LAYERS, FW])
        w2_sb = sb("w2_sb", [FW, LAYERS, FW])
        spec = sb("spec", [P, 5, 512])
        modc = sb("modc", [P, NMOD_CHUNKS, 2])
        a1 = sb("a1", [P, KD, 2])
        a2 = sb("a2", [P, KD, 2])
        ss = sb("ss", [P, 4])
        ms = sb("ms", [P, 4])
        rstd = sb("rstd", [P, 4])
        mhalf = sb("mhalf", [P, 16])
        mx = sb("mx", [P, 64])
        nm = sb("nm", [P, 64])
        lsum = sb("lsum", [P, 64])
        esink = sb("esink", [P, 4, WA_HEADS])
        esum = sb("esum", [P, 4, WA_HEADS])
        rr = sb("rr", [P, 2])
        da_ss = sb("da_ss", [P, 4, DA_HEADS])
        da_ms = sb("da_ms", [P, 4, DA_HEADS])
        da_r = sb("da_r", [P, 4, DA_HEADS])
        top_s = sb("top_s", [P, 2, TOPK])
        top_i = sb("top_i", [P, 2, TOPK], U32)
        top_f = sb("top_f", [P, 2, TOPK])
        best_s = sb("best_s", [P, TOPK])
        best_j = sb("best_j", [P, TOPK], U32)
        part_u = sb("part_u", [P, 2, TOPK], U32)
        part_f = sb("part_f", [P, 2, TOPK])
        pick = sb("pick", [P, 2, TOPK])
        nbest = sb("nbest", [P, 1])
        ebest = sb("ebest", [P, TOPK])
        esumb = sb("esumb", [P, 1])
        rbest = sb("rbest", [P, 1])
        gate = sb("gate", [P, 2, TOPK])
        idx_u = [sb(f"idx_u{b}", [P, TOPK], U32) for b in range(2)]
        idx_v = [sb(f"idx_v{b}", [P, TOPK], U32) for b in range(2)]
        dots = sb("dots", [P, 2, TOPK])
        gel = sb("gel", [P, 2, TOPK])
        wgt = sb("wgt", [P, 2, TOPK])

        bank = [ctx.enter_context(nc.psum_tensor(f"bank{b}", [P, 512], F32)) for b in range(8)]
        u_scr = nc.dram_tensor("u_scr", (LAYERS, 2, SEQ + 2, HY_COLS), F32, kind="Internal").ap()

        pe_group = sem("pe_group")
        dve_freed = sem("dve_freed")
        act_freed = sem("act_freed")
        consts_in = sem("consts_in")
        w_in_slot = [sem(f"w_in_slot{n}") for n in range(SLOTS)]
        w3_in = sem("w3_in")
        convw_in = sem("convw_in")
        hybias_in = sem("hybias_in")
        keys_in = sem("keys_in")
        fg_in = sem("fg_in")
        zrow_out = sem("zrow_out")
        u_out = sem("u_out")
        u_back = sem("u_back")
        dve_c = sem("dve_c")
        act_c = sem("act_c")
        pool_c = sem("pool_c")
        c_ready = sem("c_ready")
        c_exp = sem("c_exp")
        sin_arg = sem("sin_arg")
        sin_done = sem("sin_done")
        win_arg = sem("win_arg")
        win_done = sem("win_done")
        fsum_ready = sem("fsum_ready")
        lam_sum = sem("lam_sum")
        lam_exp = sem("lam_exp")
        mod_ready = sem("mod_ready")
        sq_ready = sem("sq_ready")
        ms_ready = sem("ms_ready")
        rstd_ready = sem("rstd_ready")
        xn_ready = sem("xn_ready")
        uprev_ready = sem("uprev_ready")
        conv_done = sem("conv_done")
        roped = sem("roped")
        y_spec = sem("y_spec")
        z_ready = sem("z_ready")
        neg_max = sem("neg_max")
        exp_done = sem("exp_done")
        comb_done = sem("comb_done")
        pv_done = sem("pv_done")
        o_taken = sem("o_taken")
        sink_arg = sem("sink_arg")
        sink_exp = sem("sink_exp")
        y_ready = sem("y_ready")
        x_done = sem("x_done")
        h2_ready = sem("h2_ready")
        sc_in = sem("sc_in")
        best_ready = sem("best_ready")
        gate_exp = sem("gate_exp")
        idx_ready = sem("idx_ready")
        idxv_ready = sem("idxv_ready")
        u_in = [sem(f"u_in{n}") for n in range(U_SLOTS)]
        v_in = [sem(f"v_in{n}") for n in range(V_SLOTS)]
        dot_done = sem("dot_done")
        gelu_done = sem("gelu_done")
        w_ready = sem("w_ready")
        diag_ready = sem("diag_ready")
        v_used = sem("v_used")
        acc_done = sem("acc_done")
        gate_r = sem("gate_r")
        gate_done = sem("gate_done")
        peer_done = sem("peer_done")
        out_ready = sem("out_ready")
        out_sent = sem("out_sent")

        freed_sem = {"dve": dve_freed, "act": act_freed}

        def wait_group(eng, key):
            eng.wait_ge(pe_group, GROUP_AT[key] + 1)

        def wait_taken(eng, key):
            n = GROUP_AT[key]
            eng.wait_ge(freed_sem[GROUPS[n][1]], FREED_COUNT[n])

        def stand_alone(eng):
            eng.nop(nofuse=True)

        def at(key):
            return bank[GROUP_AT[key] % BANKS]

        const_list = [
            (ident[:, :], A["k_ident"]), (dft_c[:, :, :], A["k_dft_c"]), (dft_s[:, :, :], A["k_dft_s"]),
            (dft_i[:, :, :], A["k_dft_i"]), (dft_cn[:, :, :], A["k_dft_cn"]), (dft_s0[:, :, :], A["k_dft_s0"]),
            (cols[:, :], A["k_cols"]), (feat[:, :], A["k_feat"]), (rope[:, :, :], A["k_rope"]),
            (mask[:, :, :], A["k_mask"]), (iota16[:, :], A["k_iota"]),
            (c_raw[:, :], A["c_cols"]), (bmod[:, :, :], A["b_mod"]), (g12[:, :, :, :], A["g12"]),
            (sinks[:, :, :], A["wa_sink"].unsqueeze(0).to_broadcast([P, LAYERS, WA_HEADS])),
            (dag[:, :, :], A["da_norm_g"].unsqueeze(0).to_broadcast([P, LAYERS, 64])),
            (fcol[:, :, :], A["fcol"]), (w1_sb[:, :, :], A["hy_w1"]), (w2_sb[:, :, :], A["hy_w2"]),
        ]
        for n, name in enumerate(("da_lq1", "da_lk1", "da_lq2", "da_lk2")):
            const_list.append((lam_v[:, n, :], A[name].rearrange("l d -> (l d)").unsqueeze(0)
                               .to_broadcast([P, LAYERS * 32])))
        for t in range(4):
            src = A["x"] if t < 2 else A["ctx"]
            const_list.append((x_res[:, t, :], src[0, (t % 2) * P:(t % 2 + 1) * P, :]))
        CONSTS = 16 * len(const_list)

        block = ctx.enter_context(nc.Block())

        @block.sync
        def _(sp):
            for dst, src in const_list:
                sp.dma_start(dst, src).then_inc(consts_in, 16)
            sp.dma_start(u_scr[:, :, 0:SEQ + 2:SEQ + 1, :], A["k_zrows"]).then_inc(zrow_out, 16)

            def load_weights(kind, l, n):
                at_n = LOAD_AT[kind, l, n]
                if at_n >= SLOTS:
                    wait_group(sp, LAST_USE[LOADS[at_n - SLOTS]])
                if kind == "mod" and l > 0 and n == 0:
                    sp.wait_ge(dot_done, TOPK * HEADS_BEFORE[l])
                    sp.wait_ge(v_used, TOPK * HEADS_BEFORE[l])
                src, width = {"mod": (A["w_mod"], 384), "in": (A["w_in"], 384),
                              "out": (A["w_out"], 256), "q": (A["peer_wq"], 256)}[kind]
                dst = wslot((kind, l, n))[:, 0:KD * width].rearrange("p (k c) -> p k c", k=KD)
                sp.dma_start(dst, src[l].rearrange("(k p) c -> p k c", p=P)[:, :, n * width:(n + 1) * width]) \
                    .then_inc(w_in_slot[at_n % SLOTS], 16)

            for l in range(LAYERS):
                if l > 0:
                    sp.wait_ge(peer_done, l)
                sp.dma_start(w3_sb, A["hy_w3"][l]).then_inc(w3_in, 16)
                sp.dma_start(f_dec, A["hy_decay"][l].unsqueeze(0).to_broadcast([P, 1024])).then_inc(w3_in, 16)
                for n in range(16):
                    load_weights("mod", l, n)
                for n in range(4):
                    load_weights("in", l, n)
                wait_group(sp, ("hT", l, KD - 1))
                for j in range(3):
                    sp.dma_start(conv_w[:, j, :], A["hy_conv_w"][l, j:j + 1, :].to_broadcast([P, HY_COLS])) \
                        .then_inc(convw_in, 16)
                sp.dma_start(conv_w[:, 3, :], A["hy_conv_b"][l:l + 1, :].to_broadcast([P, HY_COLS])) \
                    .then_inc(convw_in, 16)
                for c in range(2):
                    for t in range(q_tiles(l)):
                        wait_taken(sp, ("pj", l, c, t))
                for t in range(q_tiles(l)):
                    sp.dma_start(u_scr[l, t // 2, 1 + (t % 2) * P:1 + (t % 2 + 1) * P, :],
                                 proj[:, t, 0:HY_COLS]).then_inc(u_out, 16)
                if l == 0:
                    sp.wait_ge(zrow_out, 16)
                sp.wait_ge(u_out, 16 * sum(q_tiles(k) for k in range(l + 1)))
                for t in range(q_tiles(l)):
                    r = (t % 2) * P
                    sp.dma_start(u_prev[:, t, :], u_scr[l, t // 2, r:r + P, :]).then_inc(u_back, 16)
                    sp.dma_start(u_next[:, t, :], u_scr[l, t // 2, r + 2:r + 2 + P, :]).then_inc(u_back, 16)
                for n in range(4, 6):
                    load_weights("in", l, n)
                wait_group(sp, ("pj", l) + proj_units(l)[-1])
                sp.dma_start(hy_bias, A["hy_bias"][l].unsqueeze(0).to_broadcast([P, 2, HYW])).then_inc(hybias_in, 16)
                for n in range(4):
                    load_weights("out", l, n)
                for n in range(4):
                    load_weights("q", l, n)
                sp.wait_ge(h2_ready, l + 1)
                sp.dma_start(keysT, A["keysT"][l]).then_inc(keys_in, 16)
                for n in range(4, 8):
                    load_weights("q", l, n)
                if l == LAYERS - 1:
                    wait_group(sp, ("sc", l, 2 * HEADS - 1))
                    sp.dma_start(final_g, A["final_g"].unsqueeze(0).to_broadcast([P, D])).then_inc(fg_in, 16)
            for t in range(2):
                sp.wait_ge(out_ready, t + 1)
                sp.dma_start(out[0, t * P:(t + 1) * P, :], area_y[:, t, :]).then_inc(out_sent, 16)
            sp.wait_ge(out_sent, 32)

        @block.tensor
        def _(pe):
            def open_group(key):
                n = GROUP_AT[key]
                if n >= BANKS:
                    pe.wait_ge(freed_sem[GROUPS[n - BANKS][1]], FREED_COUNT[n - BANKS])
                return bank[n % BANKS]

            def close(ins):
                ins.then_inc(pe_group, 1)

            def weights(kind, l, n, width):
                k = LOAD_AT[kind, l, n]
                pe.wait_ge(w_in_slot[k % SLOTS], 16 * (k // SLOTS + 1))
                return wslot((kind, l, n))[:, 0:KD * width].rearrange("p (k c) -> p k c", k=KD)

            def transposes(key, blocks):
                ps = open_group(key)
                for n, src in enumerate(blocks):
                    last = nc.tensor.transpose(ps[:, n * P:(n + 1) * P], src, ident[:, :])
                close(last)

            def broadcast_rows(key, vec, s, half):
                ps = open_group(key)
                for j in range(4):
                    src = vec[:, half * 4 + j, s:s + 1]
                    last = nc.tensor.matmul(ps[:, j * P:(j + 1) * P], src.to_broadcast([P, P]), ident[:, :],
                                            start=True, stop=True)
                close(last)

            pe.wait_ge(consts_in, CONSTS)
            o_count = 0
            for l in range(LAYERS):
                T, S = q_tiles(l), streams(l)
                ps = open_group(("flt1", l))
                close(nc.tensor.matmul(ps[0:FW, 0:256], w1_sb[:, l, :], feat[:, :], start=True, stop=True))
                pe.wait_ge(sin_done, 2 * l + 1)
                ps = open_group(("flt2", l))
                close(nc.tensor.matmul(ps[0:FW, 0:256], w2_sb[:, l, :], f_z1, start=True, stop=True))
                pe.wait_ge(sin_done, 2 * l + 2)
                pe.wait_ge(w3_in, 32 * (l + 1))
                for tt in range(2):
                    for o in range(2):
                        ps = open_group(("flt3", l, tt, o))
                        close(nc.tensor.matmul(ps[:, :], f_z2[:, tt * P:(tt + 1) * P],
                                               w3_sb[:, o * 512:(o + 1) * 512], start=True, stop=True))
                pe.wait_ge(fsum_ready, 4 * (l + 1))
                for n in range(5):
                    ps = open_group(("spec", l, n))
                    mat = [dft_c[:, :, 0:P], dft_c[:, :, P:256], dft_s0[:, :, :], dft_s[:, :, P:256],
                           dft_cn[:, :, :]][n]
                    rhs = f_dif if n in (2, 3) else f_sum
                    for tt in range(2):
                        last = nc.tensor.matmul(ps[:, :], mat[:, tt, :], rhs[:, tt, :], start=tt == 0, stop=tt == 1)
                    close(last)
                pe.wait_ge(c_ready, 1)
                for n in range(16):
                    w = weights("mod", l, n, 384)
                    ps = open_group(("mod", l, n))
                    for j in range(3):
                        for kk in range(KD):
                            last = nc.tensor.matmul(ps[:, 2 * j:2 * j + 2], w[:, kk, j * P:(j + 1) * P],
                                                    c_act[:, kk, :], start=kk == 0, stop=kk == KD - 1)
                    close(last)
                pe.wait_ge(xn_ready, 4 * (l + 1))
                for kk in range(KD):
                    transposes(("hT", l, kk), [area_y[:, t, kk * P:(kk + 1) * P] for t in range(4)])
                for kk in range(KD - 2, KD):
                    wait_taken(pe, ("hT", l, kk))
                for c, t in proj_units(l):
                    w = weights("in", l, c, 384)
                    ps = open_group(("pj", l, c, t))
                    for kk in range(KD):
                        last = nc.tensor.matmul(ps[:, 0:384], hT[:, kk, t * P:(t + 1) * P], w[:, kk, :],
                                                start=kk == 0, stop=kk == KD - 1)
                    close(last)
                pe.wait_ge(roped, 2 * (l + 1))
                for t in range(2, 4):
                    for c in range(2, 6):
                        if (c, t) in proj_units(l):
                            wait_taken(pe, ("pj", l, c, t))
                for b in range(9):
                    tiles = range(4) if b in (4, 7, 8) else range(T)
                    blocks = []
                    for t in tiles:
                        if b < 4:
                            src = proj[:, t, WA0 + b * P:WA0 + (b + 1) * P]
                        elif b == 4:
                            src = proj[:, t, WA0 + 512:WA0 + 640]
                        else:
                            src = proj[:, t, DA0 + (b - 5) * P:DA0 + (b - 4) * P]
                        blocks.append(src)
                    transposes(("tr", l, b), blocks)
                pe.wait_ge(conv_done, l + 1)
                for o in range(2):
                    if o == 1:
                        pe.wait_ge(z_ready, 2 * (l + 1))
                    for m in range(2):
                        for name, mat in (("re", dft_c), ("im", dft_s)):
                            ps = open_group((name, l, o, m))
                            for tt in range(2):
                                if o == 0:
                                    z = area_p[:, :].rearrange("p (s t c) -> p s t c", s=2, t=2)[:, 0:S, tt, 512:768]
                                else:
                                    z = z_buf[:, tt, 0:S, :]
                                last = nc.tensor.matmul(ps[:, 0:S * HYW], mat[:, tt, m * P:(m + 1) * P], z,
                                                        start=tt == 0, stop=tt == 1)
                            close(last)
                    pe.wait_ge(y_spec, 4 * l + 2 * o + 2)
                    for tt in range(2):
                        ps = open_group(("inv", l, o, tt))
                        for m in range(2):
                            for mat, y in ((dft_c, yre), (dft_i, yim)):
                                last = nc.tensor.matmul(ps[:, 0:S * HYW], mat[:, m, tt * P:(tt + 1) * P],
                                                        y[:, m, 0:S * HYW], start=(m == 0 and mat is dft_c),
                                                        stop=(m == 1 and mat is dft_i))
                        close(last)
                maps = attention_maps(l)
                maps_before = sum(len(attention_maps(k)) for k in range(l))
                combs_before = sum(DA_HEADS * q_tiles(k) for k in range(l))
                wait_taken(pe, ("tr", l, 8))

                def score(n):
                    kind, t, h, m = maps[n]
                    ps = open_group(("s", l, n))
                    keys = slice(0, 512) if t < 2 else slice(256, 512)
                    width = keys.stop - keys.start
                    if kind == "wa":
                        r, b, kb = 64 * (h // 4), h % 4, 4
                        rows = slice(r, r + 64)
                    else:
                        hm = 2 * h + m
                        r, b, kb = 32 * (hm % 4), 5 + hm // 4, 7 + hm // 4
                        rows = slice(r, r + 32)
                    close(nc.tensor.matmul(ps[:, 0:width], qkT[rows, b, t * P:(t + 1) * P], qkT[rows, kb, keys],
                                           start=True, stop=True))

                def transpose_probs(n, combs):
                    kind, t, h, m = maps[n]
                    if kind == "wa":
                        pe.wait_ge(exp_done, maps_before + n + 1)
                    else:
                        pe.wait_ge(comb_done, combs_before + combs)
                    transposes(("pt", l, n), [p_buf[:, n % 4, c * P:(c + 1) * P] for c in range(4 if t < 2 else 2)])

                def times_values(n, e):
                    nonlocal o_count
                    kind, t, h, m = maps[n]
                    wait_taken(pe, ("pt", l, n))
                    if h == 0:
                        o_count += 1
                        if o_count > 2:
                            pe.wait_ge(o_taken, o_count - 2)
                    ob = bank[6 + (o_count - 1) % 2]
                    col = WA0 + 640 + 64 * (h // 4) if kind == "wa" else DA0 + 512 + 64 * h
                    chunks = list(range(4)) if t < 2 else [2, 3]
                    for i, c in enumerate(chunks):
                        last = nc.tensor.matmul(ob[:, h * 64:(h + 1) * 64], pT_buf[:, e % 2, i * P:(i + 1) * P],
                                                proj[:, c, col:col + 64], start=i == 0, stop=i == len(chunks) - 1)
                    if h == (WA_HEADS if kind == "wa" else DA_HEADS) - 1:
                        last.then_inc(pv_done, 1)

                score(0)
                score(1)
                events = []
                combs = 0
                for n, unit in enumerate(maps):
                    if n + 2 < len(maps):
                        score(n + 2)
                    if has_pv(unit):
                        if unit[0] == "da":
                            combs += 1
                        transpose_probs(n, combs)
                        events.append(n)
                        if len(events) > 1:
                            times_values(events[-2], len(events) - 2)
                times_values(events[-1], len(events) - 1)
                pe.wait_ge(y_ready, l + 1)
                for v in range(3):
                    for s in range(S):
                        for half in range(2):
                            vec = [modc[:, 2 * KD:3 * KD, :], a2[:, :, :], modc[:, 3 * KD:4 * KD, :]][v]
                            broadcast_rows(("bc", l, v, s, half), vec, s, half)
                for kk in range(KD):
                    transposes(("yT", l, kk), [area_y[:, t, kk * P:(kk + 1) * P] for t in range(T)])
                for kk in range(KD - 2, KD):
                    wait_taken(pe, ("yT", l, kk))
                for n in range(4):
                    w = weights("out", l, n, 256)
                    for t in range(T):
                        ps = open_group(("wo", l, n, t))
                        for kk in range(KD):
                            last = nc.tensor.matmul(ps[:, 0:256], hT[:, kk, t * P:(t + 1) * P], w[:, kk, :],
                                                    start=kk == 0, stop=kk == KD - 1)
                        close(last)
                pe.wait_ge(h2_ready, l + 1)
                for kk in range(KD):
                    transposes(("h2T", l, kk), [area_y[:, t, kk * P:(kk + 1) * P] for t in range(T)])
                for kk in range(KD - 2, KD):
                    wait_taken(pe, ("h2T", l, kk))
                pe.wait_ge(keys_in, 16 * (l + 1))
                for hp in range(2 * HEADS):
                    w = weights("q", l, hp // 2, 256)
                    c = (hp % 2) * P
                    ps = open_group(("q", l, hp))
                    for kk in range(KD):
                        last = nc.tensor.matmul(ps[:, 0:T * P], w[:, kk, c:c + P], hT[:, kk, 0:T * P],
                                                start=kk == 0, stop=kk == KD - 1)
                    close(last)
                    wait_taken(pe, ("q", l, hp))
                    ps = open_group(("sc", l, hp))
                    for t in range(T):
                        last = nc.tensor.matmul(ps[:, t * P:(t + 1) * P], qT[:, hp % 2, t * P:(t + 1) * P],
                                                keysT[:, hp, :], start=True, stop=True)
                    close(last)
                for s in range(S):
                    for half in range(2):
                        broadcast_rows(("bc5", l, s, half), modc[:, 5 * KD:6 * KD, :], s, half)

                base = HEADS_BEFORE[l]
                NH = HEADS * T

                def v_head(g, b, first):
                    if not first:
                        pe.wait_ge(acc_done, (g + (base - 1)) * 2)
                    for j in range(TOPK):
                        pe.wait_ge(v_in[j % V_SLOTS], (g + base) * 64 + 16 * (j // V_SLOTS) + 16)
                        pe.wait_ge(diag_ready, (g + base) * TOPK + j + 1)
                        for half in range(2):
                            last = nc.tensor.matmul(bank[2 * b + half][:, :], diag[:, j % G_SLOTS, :],
                                                    v_rows[j % V_SLOTS][:, half * 512:(half + 1) * 512],
                                                    start=j == 0, stop=j == TOPK - 1)
                        last.then_inc(v_used, 1)

                for s in range(S):
                    for half in range(2):
                        wait_taken(pe, ("bc5", l, s, half))
                wait_taken(pe, ("sc", l, 2 * HEADS - 1))
                v_head(0, 0, True)
                v_head(1, 1, True)
                with pe.Fori(1, NH // 2 - 1) as i:
                    v_head(i * 2, 0, False)
                    v_head(i * 2 + 1, 1, False)
                v_head(NH - 2, 0, False)
                v_head(NH - 1, 1, False)
                pe.wait_ge(acc_done, 2 * (base + NH))

        @block.scalar
        def _(act):
            chained = [0]

            def chain(ins):
                chained[0] += 1
                ins.then_inc(act_c, 1)
                act.wait_ge(act_c, chained[0])

            def freed(ins):
                ins.then_inc(act_freed, 1)

            act.wait_ge(consts_in, CONSTS)
            nc.scalar.activation(c_tmp[:, :], c_raw[:, :], ACT.Exp, scale=-1.0).then_inc(c_exp, 1)
            act.wait_ge(lam_sum, 1)
            nc.scalar.activation(lam_s[:, :, :], lam_s[:, :, :], ACT.Exp).then_inc(lam_exp, 1)
            for l in range(LAYERS):
                T, S = q_tiles(l), streams(l)
                for n, z in enumerate((f_z1, f_z2)):
                    act.wait_ge(sin_arg, 2 * l + n + 1)
                    nc.scalar.activation(z, f_arg, ACT.Sin).then_inc(sin_done, 1)
                act.wait_ge(win_arg, l + 1)
                for tt in range(2):
                    if tt:
                        act.wait_ge(fsum_ready, 4 * l + 2)
                    nc.scalar.activation(f_win, f_dec, ACT.Exp, scale=cols[:, tt:tt + 1]).then_inc(win_done, 1)
                for n in range(5):
                    wait_group(act, ("spec", l, n))
                    scale = cols[:, 4:5] if n in (0, 2, 4) else cols[:, 5:6]
                    freed(nc.scalar.activation(spec[:, n, :], at(("spec", l, n))[:, :], ACT.Copy, scale=scale))
                if l > 0:
                    act.wait_ge(peer_done, l)
                for t in range(4):
                    ins = nc.scalar.activation(junk, x_res[:, t, :], ACT.Square, accum_out=ss[:, t:t + 1])
                    if t < 3:
                        chain(ins)
                ins.then_inc(sq_ready, 1)
                act.wait_ge(mod_ready, l + 1)
                for kk in range(1, KD, 2):
                    wait_group(act, ("hT", l, kk))
                    for s in range(2):
                        ins = nc.scalar.activation(hT[:, kk, s * 256:(s + 1) * 256],
                                                   at(("hT", l, kk))[:, s * 256:(s + 1) * 256], ACT.Identity,
                                                   bias=modc[:, kk, s:s + 1], scale=a1[:, kk, s:s + 1])
                    freed(ins)
                for c, t in proj_units(l):
                    if t % 2 == 1:
                        wait_group(act, ("pj", l, c, t))
                        freed(nc.scalar.activation(proj[:, t, c * 384:(c + 1) * 384],
                                                   at(("pj", l, c, t))[:, 0:384], ACT.Copy))
                for b in range(9):
                    wait_group(act, ("tr", l, b))
                    width = 512 if b in (4, 7, 8) else T * P
                    freed(nc.scalar.activation(qkT[:, b, 0:width], at(("tr", l, b))[:, 0:width], ACT.Copy))
                maps = attention_maps(l)
                maps_before = sum(len(attention_maps(k)) for k in range(l))

                def exps(n):
                    kind, t, h, m = maps[n]
                    c = stat_column(*maps[n])
                    act.wait_ge(neg_max, maps_before + n + 1)
                    width = 512 if t < 2 else 256
                    masked = kind == "wa" and t < 2
                    src = p_buf[:, n % 4, 0:width] if masked else at(("s", l, n))[:, 0:width]
                    if not masked:
                        wait_group(act, ("s", l, n))
                    ins = nc.scalar.activation(p_buf[:, n % 4, 0:width], src, ACT.Exp, bias=nm[:, c:c + 1],
                                               scale=WA_SCALE if kind == "wa" else DA_SCALE,
                                               accum_out=lsum[:, c:c + 1])
                    ins.then_inc(exp_done, 1)
                    if not masked:
                        act.wait_ge(exp_done, maps_before + n + 1)
                        act.sem_inc(act_freed, 1)

                exps(0)
                e = 0
                for n, unit in enumerate(maps):
                    if n + 1 < len(maps):
                        exps(n + 1)
                    if has_pv(unit):
                        if GROUPS[GROUP_AT["pt", l, n]][1] == "act":
                            wait_group(act, ("pt", l, n))
                            width = 512 if unit[1] < 2 else 256
                            freed(nc.scalar.activation(pT_buf[:, e % 2, 0:width],
                                                       at(("pt", l, n))[:, 0:width], ACT.Copy))
                        e += 1
                act.wait_ge(sink_arg, l + 1)
                nc.scalar.activation(esink[:, 0:T, :], esink[:, 0:T, :], ACT.Exp).then_inc(sink_exp, 1)
                for v in range(3):
                    for s in range(S):
                        wait_group(act, ("bc", l, v, s, 1))
                        dst = (gate_bc, a2_bc, b2_bc)[v]
                        freed(nc.scalar.activation(dst[:, s, 512:1024], at(("bc", l, v, s, 1))[:, :], ACT.Copy))
                for kk in range(1, KD, 2):
                    wait_group(act, ("yT", l, kk))
                    freed(nc.scalar.activation(hT[:, kk, 0:T * P], at(("yT", l, kk))[:, 0:T * P], ACT.Copy))
                act.wait_ge(x_done, l + 1)
                for t in range(T):
                    ins = nc.scalar.activation(junk, x_res[:, t, :], ACT.Square, accum_out=ss[:, t:t + 1])
                    if t < T - 1:
                        chain(ins)
                ins.then_inc(sq_ready, 1)
                for kk in range(1, KD, 2):
                    wait_group(act, ("h2T", l, kk))
                    freed(nc.scalar.activation(hT[:, kk, 0:T * P], at(("h2T", l, kk))[:, 0:T * P], ACT.Copy))
                for hp in range(2 * HEADS):
                    wait_group(act, ("q", l, hp))
                    if hp >= 2:
                        wait_group(act, ("sc", l, hp - 2))
                    freed(nc.scalar.activation(qT[:, hp % 2, 0:T * P], at(("q", l, hp))[:, 0:T * P], ACT.Copy))
                for s in range(S):
                    wait_group(act, ("bc5", l, s, 1))
                    freed(nc.scalar.activation(gate_bc[:, s, 512:1024], at(("bc5", l, s, 1))[:, :], ACT.Copy))
                base = HEADS_BEFORE[l]
                NH = HEADS * T

                def copy_scores(g, b):
                    act.wait_ge(idx_ready, g + (base - 1))
                    nc.scalar.activation(head_sc[:, b, :, :].rearrange("p a k -> p (a k)"),
                                         scores[:, bass.ds(g * 256, 256)], ACT.Copy).then_inc(sc_in, 1)

                def gate_exps(g):
                    act.wait_ge(best_ready, g + (base + 1))
                    nc.scalar.activation(ebest[:, :], best_s[:, :], ACT.Exp, bias=nbest[:, 0:1],
                                         accum_out=esumb[:, 0:1]).then_inc(gate_exp, 1)

                def gelu(g, b):
                    act.wait_ge(dot_done, (g + base) * TOPK + TOPK)
                    nc.scalar.activation(gel[:, b, :], dots[:, b, :], ACT.Gelu).then_inc(gelu_done, 1)

                def diagonals(g, b, js, first=False):
                    act.wait_ge(w_ready, g + (base + 1))
                    for j in js:
                        if not (first and base == 0 and j < G_SLOTS):
                            act.wait_ge(v_used, (g + base) * TOPK + j - G_SLOTS + 1)
                        nc.scalar.activation(diag[:, j % G_SLOTS, :], ident[:, :], ACT.Copy,
                                             scale=wgt[:, b, j:j + 1]).then_inc(diag_ready, 1)

                def step(g, b, first=False, last=False):
                    if not last:
                        copy_scores(g + 1, 1 - b)
                    diagonals(g - 1, 1 - b, range(TOPK // 2), first)
                    if not last:
                        gate_exps(g + 1)
                    diagonals(g - 1, 1 - b, range(TOPK // 2, TOPK))
                    gelu(g, b)

                if l == 0:
                    for hp in (2 * HEADS - 1,):
                        wait_taken(act, ("sc", l, hp))
                    nc.scalar.activation(head_sc[:, 0, :, :].rearrange("p a k -> p (a k)"),
                                         scores[:, 0:256], ACT.Copy).then_inc(sc_in, 1)
                else:
                    wait_taken(act, ("sc", l, 2 * HEADS - 1))
                    copy_scores(0, 0)
                gate_exps(0)
                if l == 0:
                    nc.scalar.activation(head_sc[:, 1, :, :].rearrange("p a k -> p (a k)"),
                                         scores[:, 256:512], ACT.Copy).then_inc(sc_in, 1)
                else:
                    copy_scores(1, 1)
                gate_exps(1)
                gelu(0, 0)
                step(1, 1, first=True)
                with act.Fori(1, NH // 2 - 1) as i:
                    step(i * 2, 0)
                    step(i * 2 + 1, 1)
                step(NH - 2, 0)
                step(NH - 1, 1, last=True)
                diagonals(NH - 1, 1, range(TOPK))
            act.wait_ge(peer_done, LAYERS)
            for t in range(2):
                ins = nc.scalar.activation(junk, x_res[:, t, :], ACT.Square, accum_out=ss[:, t:t + 1])
                if t == 0:
                    chain(ins)
            ins.then_inc(sq_ready, 1)

        @block.gpsimd
        def _(pool):
            nc.gpsimd.memset(mhalf[:, :], -0.5).then_inc(pool_c, 1)
            pool.wait_ge(pool_c, 1)

            def rsqrt(n_ms, n_rstd, count):
                pool.wait_ge(ms_ready, n_ms)
                nc.gpsimd.tensor_tensor(rstd[:, 0:count], ms[:, 0:count], mhalf[:, 0:count], ALU.pow) \
                    .then_inc(rstd_ready, 1)

            for l in range(LAYERS):
                T = q_tiles(l)
                rsqrt(3 * l + 1, 3 * l + 1, 4)
                pool.wait_ge(convw_in, 64 * (l + 1))
                pool.wait_ge(u_back, 32 * sum(q_tiles(k) for k in range(l + 1)))
                for buf, j in ((u_prev, 0), (u_next, 2)):
                    for t in range(T):
                        nc.gpsimd.tensor_tensor(buf[:, t, :], buf[:, t, :], conv_w[:, j, :], ALU.mult) \
                            .then_inc(uprev_ready, 1)
                pool.wait_ge(ms_ready, 3 * l + 2)
                nc.gpsimd.tensor_tensor(da_r[:, 0:T, :].rearrange("p t h -> p (t h)"),
                                        da_ms[:, 0:T, :].rearrange("p t h -> p (t h)"),
                                        mhalf[:, 0:T * DA_HEADS], ALU.pow).then_inc(rstd_ready, 1)
                rsqrt(3 * l + 3, 3 * l + 3, T)
                base = HEADS_BEFORE[l]
                NH = HEADS * T
                wait_group(pool, ("sc", l, 2 * HEADS - 1))

                def gather_u(g, b, j, first=False):
                    if not (first and j < U_SLOTS):
                        pool.wait_ge(dot_done, (g + base) * TOPK + j - U_SLOTS + 1)
                    stand_alone(pool)
                    pool.indirect_dma_start(u_rows[j % U_SLOTS], None, A["peer_u"],
                                            bass.IndirectOffsetOnAxis(idx_u[b][:, j:j + 1], 0)) \
                        .then_inc(u_in[j % U_SLOTS], 16)

                def gather_v(g, b, j, first=False):
                    if not (first and j < V_SLOTS):
                        pool.wait_ge(v_used, (g + base) * TOPK + j - V_SLOTS + 1)
                    stand_alone(pool)
                    pool.indirect_dma_start(v_rows[j % V_SLOTS], None, A["peer_v"],
                                            bass.IndirectOffsetOnAxis(idx_v[b][:, j:j + 1], 0)) \
                        .then_inc(v_in[j % V_SLOTS], 16)

                def step(g, b, first=False):
                    pool.wait_ge(idx_ready, g + (base + 1))
                    pool.wait_ge(idxv_ready, g + base)
                    for j in range(TOPK):
                        gather_u(g, b, j)
                        gather_v(g - 1, 1 - b, j, first)

                pool.wait_ge(idx_ready, base + 1)
                for j in range(TOPK):
                    gather_u(0, 0, j, True)
                step(1, 1, True)
                with pool.Fori(1, NH // 2) as i:
                    step(i * 2, 0)
                    step(i * 2 + 1, 1)
                pool.wait_ge(idxv_ready, base + NH)
                for j in range(TOPK):
                    gather_v(NH - 1, 1, j)
            rsqrt(3 * LAYERS + 1, 3 * LAYERS + 1, 2)

        @block.vector
        def _(dve):
            V = nc.vector
            counts = {}

            def done(ins, signal=dve_c):
                counts[signal.name] = counts.get(signal.name, 0) + 1
                ins.then_inc(signal, 1)
                dve.wait_ge(signal, counts[signal.name])

            def freed(ins):
                done(ins, dve_freed)

            dve.wait_ge(consts_in, CONSTS)
            dve.wait_ge(c_exp, 1)
            done(V.tensor_scalar(c_tmp[:, :], c_tmp[:, :], 1.0, None, ALU.add))
            done(V.reciprocal(c_tmp[:, :], c_tmp[:, :]))
            done(V.tensor_tensor(c_act[:, :, :].rearrange("p k s -> p (k s)"), c_raw[:, :], c_tmp[:, :], ALU.mult),
                 c_ready)
            for n in range(2):
                done(V.tensor_tensor(lam_p[:, n, :], lam_v[:, 2 * n, :], lam_v[:, 2 * n + 1, :], ALU.mult))
            done(V.tensor_reduce(lam_s[:, :, :].rearrange("p a l -> p (a l)"),
                                 lam_p[:, :, :].rearrange("p a (l d) -> p (a l) d", l=LAYERS), AX, ALU.add), lam_sum)
            dve.wait_ge(lam_exp, 1)
            done(V.tensor_tensor(lam_n[:, :], lam_s[:, 1, :], lam_s[:, 0, :], ALU.subtract))
            for l in range(LAYERS):
                done(V.tensor_scalar(lam_n[:, l:l + 1], lam_n[:, l:l + 1], -lam_init_of(l), None, ALU.add))
                done(V.tensor_scalar(dag[:, l, :], dag[:, l, :], 1.0 - lam_init_of(l), None, ALU.mult))
            done(V.tensor_scalar(nsinks[:, :, :], sinks[:, :, :], -1.0, None, ALU.mult))
            sq_count = 0
            rstd_count = 0
            o_count = 0

            def mean_square(count):
                nonlocal sq_count, rstd_count
                sq_count += 1
                dve.wait_ge(sq_ready, sq_count)
                done(V.tensor_scalar(ms[:, 0:count], ss[:, 0:count], 1.0 / D, EPS, ALU.mult, ALU.add), ms_ready)
                rstd_count += 1
                dve.wait_ge(rstd_ready, rstd_count)

            for l in range(LAYERS):
                T, S = q_tiles(l), streams(l)
                dve.wait_ge(w3_in, 32 * (l + 1))
                done(V.scalar_tensor_tensor(f_dec, f_dec, -1.0, f_dec, ALU.mult, ALU.max), win_arg)
                for n, key in enumerate((("flt1", l), ("flt2", l))):
                    wait_group(dve, key)
                    if n:
                        dve.wait_ge(sin_done, 2 * l + 1)
                    freed(V.tensor_scalar(f_arg, at(key)[0:FW, 0:256], fcol[:, l, 1 + n:2 + n], fcol[:, l, 0:1],
                                          ALU.add, ALU.mult))
                    done(V.tensor_scalar(f_rnd, f_arg, 1.0 / (2.0 * math.pi), ROUND, ALU.mult, ALU.add))
                    done(V.tensor_scalar(f_rnd, f_rnd, -ROUND, None, ALU.add))
                    done(V.scalar_tensor_tensor(f_arg, f_rnd, -C1, f_arg, ALU.mult, ALU.add))
                    done(V.scalar_tensor_tensor(f_arg, f_rnd, -C2, f_arg, ALU.mult, ALU.add))
                    done(V.tensor_scalar(f_arg, f_arg, PI_IN, -PI_IN, ALU.min, ALU.max), sin_arg)
                for tt in range(2):
                    dve.wait_ge(win_done, 2 * l + tt + 1)
                    for o in range(2):
                        key = ("flt3", l, tt, o)
                        wait_group(dve, key)
                        freed(V.tensor_tensor(f_hw, at(key)[:, :], f_win[:, o * 512:(o + 1) * 512], ALU.mult))
                        c = slice(o * HYW, (o + 1) * HYW)
                        done(V.tensor_scalar(f_hw[:, HYW:512], f_hw[:, HYW:512], cols[:, 2 + tt:3 + tt], None,
                                             ALU.mult))
                        done(V.tensor_tensor(f_sum[:, tt, c], f_hw[:, 0:HYW], f_hw[:, HYW:512], ALU.add))
                        done(V.tensor_tensor(f_dif[:, tt, c], f_hw[:, 0:HYW], f_hw[:, HYW:512], ALU.subtract),
                             fsum_ready)
                mean_square(4)
                for t in range(4):
                    done(V.tensor_scalar(area_y[:, t, :], x_res[:, t, :], rstd[:, t:t + 1], None, ALU.mult), xn_ready)
                for n in range(16):
                    key = ("mod", l, n)
                    wait_group(dve, key)
                    freed(V.tensor_tensor(modc[:, 3 * n:3 * n + 3, :],
                                          at(key)[:, 0:6].rearrange("p (j s) -> p j s", s=2),
                                          bmod[:, l, 3 * n:3 * n + 3].unsqueeze(2).to_broadcast([P, 3, 2]), ALU.add))
                for n, (dst, c) in enumerate(((a1, KD), (a2, 4 * KD))):
                    ins = V.scalar_tensor_tensor(dst[:, :, :], modc[:, c:c + KD, :], 1.0,
                                                 g12[:, l, n, :].unsqueeze(2).to_broadcast([P, KD, 2]),
                                                 ALU.add, ALU.mult)
                    done(ins, mod_ready if n else dve_c)
                for kk in range(0, KD, 2):
                    wait_group(dve, ("hT", l, kk))
                    for s in range(2):
                        ins = V.tensor_scalar(hT[:, kk, s * 256:(s + 1) * 256],
                                              at(("hT", l, kk))[:, s * 256:(s + 1) * 256],
                                              a1[:, kk, s:s + 1], modc[:, kk, s:s + 1], ALU.mult, ALU.add)
                        (freed if s else done)(ins)

                def conv():
                    dve.wait_ge(convw_in, 64 * (l + 1))
                    for t in range(T):
                        for c in range(2):
                            wait_taken(dve, ("pj", l, c, t))
                    dve.wait_ge(u_back, 32 * sum(q_tiles(k) for k in range(l + 1)))
                    hy = proj[:, 0:T, 0:HY_COLS]

                    def tap(j):
                        return conv_w[:, j:j + 1, :].to_broadcast([P, T, HY_COLS])
                    done(V.tensor_tensor(hy, hy, tap(1), ALU.mult))
                    done(V.tensor_tensor(hy, hy, tap(3), ALU.add))
                    dve.wait_ge(uprev_ready, 2 * sum(q_tiles(k) for k in range(l + 1)))
                    done(V.tensor_tensor(hy, hy, u_prev[:, 0:T, :], ALU.add))
                    done(V.tensor_tensor(hy, hy, u_next[:, 0:T, :], ALU.add), conv_done)

                for c, t in proj_units(l):
                    if t % 2 == 0:
                        wait_group(dve, ("pj", l, c, t))
                        freed(V.tensor_copy(proj[:, t, c * 384:(c + 1) * 384], at(("pj", l, c, t))[:, 0:384]))
                conv()
                for t in range(2):
                    for c in range(2, 6):
                        wait_taken(dve, ("pj", l, c, t))
                    for first_col, heads, dim, r0 in ((WA0, 10, 64, 0), (DA0, 16, 32, 128)):
                        m = dim // 4
                        xv = proj[:, t, first_col:first_col + heads * dim].rearrange("p (h d) -> p h d", d=dim)
                        x4 = proj[:, t, first_col:first_col + heads * dim] \
                            .rearrange("p (h a b m) -> p h a b m", a=2, b=2, m=m)
                        t1 = rope_1[:, 0:heads * dim].rearrange("p (h d) -> p h d", d=dim)
                        t2 = rope_2[:, 0:heads * dim].rearrange("p (h d) -> p h d", d=dim)
                        t4 = rope_2[:, 0:heads * dim].rearrange("p (h a b m) -> p h a b m", a=2, b=2, m=m)
                        cos = rope[:, t, r0:r0 + dim].unsqueeze(1).to_broadcast([P, heads, dim])
                        sin = rope[:, t, r0 + dim:r0 + 2 * dim].rearrange("p (a b m) -> p a b m", a=2, b=2)
                        done(V.tensor_tensor(t1, xv, cos, ALU.mult))
                        for half in range(2):
                            done(V.tensor_tensor(t4[:, :, :, half, :], x4[:, :, :, 1 - half, :],
                                                 sin[:, :, half, :].unsqueeze(1).to_broadcast([P, heads, 2, m]),
                                                 ALU.mult))
                        done(V.tensor_tensor(xv, t1, t2, ALU.add), roped if first_col == DA0 else dve_c)
                dve.wait_ge(hybias_in, 16 * (l + 1))
                for k in range(5):
                    wait_taken(dve, ("spec", l, k))
                W = S * HYW

                def sv(ap):
                    return ap[:, 0:W].rearrange("p (s c) -> p s c", c=HYW)

                for o in range(2):
                    for m in range(2):
                        re, im = at(("re", l, o, m)), at(("im", l, o, m))
                        h = [spec[:, k, o * HYW:(o + 1) * HYW].unsqueeze(1).to_broadcast([P, S, HYW])
                             for k in (m, 2 + m, 4 if m == 0 else 1)]
                        wait_group(dve, ("im", l, o, m))
                        done(V.tensor_tensor(sv(yre[:, m, :]), sv(re), h[0], ALU.mult))
                        done(V.tensor_tensor(sv(hy_tmp), sv(im), h[1], ALU.mult))
                        done(V.tensor_tensor(yre[:, m, 0:W], yre[:, m, 0:W], hy_tmp[:, 0:W], ALU.subtract))
                        freed(V.tensor_tensor(sv(yim[:, m, :]), sv(re), h[1], ALU.mult))
                        freed(V.tensor_tensor(sv(hy_tmp), sv(im), h[2], ALU.mult))
                        done(V.tensor_tensor(yim[:, m, 0:W], yim[:, m, 0:W], hy_tmp[:, 0:W], ALU.add), y_spec)
                    for tt in range(2):
                        key = ("inv", l, o, tt)
                        pj = area_p[:, :].rearrange("p (s t c) -> p s t c", s=2, t=2)
                        z = pj[:, 0:S, tt, 512:768] if o == 0 else z_buf[:, tt, 0:S, :]
                        wait_group(dve, key)
                        done(V.tensor_tensor(sv(hy_tmp), z, hy_bias[:, o:o + 1, :].to_broadcast([P, S, HYW]),
                                             ALU.mult))
                        freed(V.tensor_tensor(hy_tmp[:, 0:W], hy_tmp[:, 0:W], at(key)[:, 0:W], ALU.add))
                        dst = z_buf[:, tt, 0:S, :] if o == 0 else \
                            area_y[:, :, :].rearrange("p (s t) c -> p s t c", s=2)[:, 0:S, tt, 0:HYW]
                        done(V.tensor_tensor(dst, sv(hy_tmp), pj[:, 0:S, tt, o * HYW:(o + 1) * HYW], ALU.mult),
                             z_ready if o == 0 else dve_c)
                maps = attention_maps(l)
                maps_before = sum(len(attention_maps(k)) for k in range(l))

                def stats(n):
                    kind, t, h, m = maps[n]
                    c = stat_column(*maps[n])
                    key = ("s", l, n)
                    wait_group(dve, key)
                    width = 512 if t < 2 else 256
                    if kind == "wa" and t < 2:
                        freed(V.tensor_tensor_reduce(out=p_buf[:, n % 4, :], in0=at(key)[:, :], in1=mask[:, t, :],
                                                     scale=1.0, scalar=LOW, op0=ALU.add, op1=ALU.max,
                                                     accum_out=mx[:, c:c + 1]))
                    else:
                        done(V.tensor_reduce(mx[:, c:c + 1], at(key)[:, 0:width], AX, ALU.max))
                    if kind == "wa":
                        done(V.tensor_scalar(nm[:, c:c + 1], mx[:, c:c + 1], -WA_SCALE, nsinks[:, l, h:h + 1],
                                             ALU.mult, ALU.min), neg_max)
                    else:
                        done(V.tensor_scalar(nm[:, c:c + 1], mx[:, c:c + 1], -DA_SCALE, None, ALU.mult), neg_max)

                def combine(n):
                    kind, t, h, m = maps[n]
                    c = stat_column(*maps[n])
                    width = 512 if t < 2 else 256
                    dve.wait_ge(exp_done, maps_before + n + 1)
                    done(V.reciprocal(rr[:, :], lsum[:, c - 1:c + 1]))
                    done(V.tensor_tensor(rr[:, 1:2], rr[:, 1:2], lam_n[:, l:l + 1], ALU.mult))
                    p0, p1 = p_buf[:, (n - 1) % 4, 0:width], p_buf[:, n % 4, 0:width]
                    done(V.tensor_scalar(p1, p1, rr[:, 1:2], None, ALU.mult))
                    done(V.scalar_tensor_tensor(p1, p0, rr[:, 0:1], p1, ALU.mult, ALU.add), comb_done)

                def take_outputs(n):
                    nonlocal o_count
                    kind, t, h, m = maps[n]
                    o_count += 1
                    dve.wait_ge(pv_done, o_count)
                    width, c = (512, 256) if kind == "wa" else (256, 768)
                    done(V.tensor_copy(area_y[:, t, c:c + width], bank[6 + (o_count - 1) % 2][:, 0:width]), o_taken)

                stats(0)
                stats(1)
                finished = None
                e = 0
                for n, unit in enumerate(maps):
                    if n + 2 < len(maps):
                        stats(n + 2)
                    if has_pv(unit):
                        if unit[0] == "da":
                            combine(n)
                        if GROUPS[GROUP_AT["pt", l, n]][1] == "dve":
                            wait_group(dve, ("pt", l, n))
                            width = 512 if unit[1] < 2 else 256
                            freed(V.tensor_copy(pT_buf[:, e % 2, 0:width], at(("pt", l, n))[:, 0:width]))
                        e += 1
                        if finished is not None:
                            take_outputs(finished)
                            finished = None
                        if unit[2] == (WA_HEADS if unit[0] == "wa" else DA_HEADS) - 1:
                            finished = n
                take_outputs(finished)
                dve.wait_ge(exp_done, maps_before + len(maps))
                done(V.tensor_tensor(esink[:, 0:T, :], nm[:, 0:T * WA_HEADS].rearrange("p (t h) -> p t h", t=T),
                                     sinks[:, l:l + 1, :].to_broadcast([P, T, WA_HEADS]), ALU.add), sink_arg)
                da = area_y[:, 0:T, 768:1024]
                done(V.tensor_tensor(da_sq[:, 0:T, :], da, da, ALU.mult))
                for t in range(T):
                    done(V.tensor_reduce(da_ss[:, t, :], da_sq[:, t, :].rearrange("p (h d) -> p h d", d=64), AX,
                                         ALU.add))
                done(V.tensor_scalar(da_ms[:, 0:T, :], da_ss[:, 0:T, :], 1.0 / 64, EPS, ALU.mult, ALU.add), ms_ready)
                dve.wait_ge(sink_exp, l + 1)
                done(V.tensor_tensor(esum[:, 0:T, :], esink[:, 0:T, :],
                                     lsum[:, 0:T * WA_HEADS].rearrange("p (t h) -> p t h", t=T), ALU.add))
                done(V.reciprocal(esum[:, 0:T, :], esum[:, 0:T, :]))
                for t in range(T):
                    wa = area_y[:, t, 256:768].rearrange("p (h d) -> p h d", d=64)
                    done(V.tensor_tensor(wa, wa, esum[:, t, :].unsqueeze(2).to_broadcast([P, WA_HEADS, 64]), ALU.mult))
                rstd_count += 1
                dve.wait_ge(rstd_ready, rstd_count)
                for t in range(T):
                    dh = area_y[:, t, 768:1024].rearrange("p (h d) -> p h d", d=64)
                    done(V.tensor_tensor(dh, dh, da_r[:, t, :].unsqueeze(2).to_broadcast([P, DA_HEADS, 64]), ALU.mult))
                    done(V.tensor_tensor(dh, dh, dag[:, l:l + 1, :].to_broadcast([P, DA_HEADS, 64]), ALU.mult),
                         y_ready if t == T - 1 else dve_c)
                for v in range(3):
                    for s in range(S):
                        wait_group(dve, ("bc", l, v, s, 0))
                        dst = (gate_bc, a2_bc, b2_bc)[v]
                        freed(V.tensor_copy(dst[:, s, 0:512], at(("bc", l, v, s, 0))[:, :]))
                for kk in range(0, KD, 2):
                    wait_group(dve, ("yT", l, kk))
                    freed(V.tensor_copy(hT[:, kk, 0:T * P], at(("yT", l, kk))[:, 0:T * P]))
                for s in range(S):
                    wait_taken(dve, ("bc", l, 0, s, 1))
                for n in range(4):
                    for t in range(T):
                        key = ("wo", l, n, t)
                        c = slice(n * 256, (n + 1) * 256)
                        wait_group(dve, key)
                        freed(V.tensor_tensor(res_tmp, at(key)[:, 0:256], gate_bc[:, t // 2, c], ALU.mult))
                        done(V.tensor_tensor(x_res[:, t, c], x_res[:, t, c], res_tmp, ALU.add),
                             x_done if (n, t) == (3, T - 1) else dve_c)
                mean_square(T)
                for s in range(S):
                    wait_taken(dve, ("bc", l, 2, s, 1))
                for t in range(T):
                    done(V.scalar_tensor_tensor(area_y[:, t, :], x_res[:, t, :], rstd[:, t:t + 1],
                                                a2_bc[:, t // 2, :], ALU.mult, ALU.mult))
                    done(V.tensor_tensor(area_y[:, t, :], area_y[:, t, :], b2_bc[:, t // 2, :], ALU.add),
                         h2_ready if t == T - 1 else dve_c)
                for kk in range(0, KD, 2):
                    wait_group(dve, ("h2T", l, kk))
                    freed(V.tensor_copy(hT[:, kk, 0:T * P], at(("h2T", l, kk))[:, 0:T * P]))
                sc4 = scores.rearrange("p (t h k) -> p t h k", t=4, h=16)
                for hp in range(2 * HEADS):
                    wait_group(dve, ("sc", l, hp))
                    freed(V.tensor_copy(sc4[:, 0:T, hp, :],
                                        at(("sc", l, hp))[:, 0:T * P].rearrange("p (t k) -> p t k", k=P)))
                for s in range(S):
                    wait_group(dve, ("bc5", l, s, 0))
                    freed(V.tensor_copy(gate_bc[:, s, 0:512], at(("bc5", l, s, 0))[:, :]))
                done(V.memset(o_acc[:, 0:T, :], 0.0))

                base = HEADS_BEFORE[l]
                NH = HEADS * T
                CH = 27
                chain0 = counts.get(dve_c.name, 0)

                def top_k(g, b):
                    k = [0]

                    def link(ins):
                        k[0] += 1
                        ins.then_inc(dve_c, 1)
                        dve.wait_ge(dve_c, g * CH + (chain0 + k[0]))
                        if k[0] in (1, 2, 3, 4, 5, 6, 7, 8, 9, 12, 13, 14, 15, 16):
                            stand_alone(dve)

                    dve.wait_ge(sc_in, g + (base + 1))
                    stand_alone(dve)
                    for a in range(2):
                        src = head_sc[:, b, a, :]
                        link(V.max(top_s[:, a, 0:8], src))
                        link(V.max_index(top_i[:, a, 0:8], top_s[:, a, 0:8], src))
                        link(V.match_replace(sc_left[:, a, :], top_s[:, a, 0:8], src, LOW))
                        link(V.max(top_s[:, a, 8:16], sc_left[:, a, :]))
                        link(V.max_index(top_i[:, a, 8:16], top_s[:, a, 8:16], sc_left[:, a, :]))
                    link(V.tensor_copy(top_f[:, :, :], top_i[:, :, :]))
                    c3 = cand.rearrange("p (a b) -> p a b", a=TOPK)
                    link(V.tensor_tensor(c3, top_s[:, 0, :].unsqueeze(2).to_broadcast([P, TOPK, TOPK]),
                                         top_s[:, 1, :].unsqueeze(1).to_broadcast([P, TOPK, TOPK]), ALU.add))
                    link(V.max(best_s[:, 0:8], cand))
                    link(V.match_replace(cand2, best_s[:, 0:8], cand, LOW))
                    link(V.max(best_s[:, 8:16], cand2))
                    ins = V.tensor_scalar(nbest[:, :], best_s[:, 0:1], -1.0, None, ALU.mult)
                    ins.then_inc(best_ready, 1)
                    link(V.max_index(best_j[:, 0:8], best_s[:, 0:8], cand))
                    link(V.max_index(best_j[:, 8:16], best_s[:, 8:16], cand2))
                    link(V.tensor_scalar(part_u[:, 0, :], best_j[:, :], 4, None, ALU.logical_shift_right))
                    link(V.tensor_scalar(part_u[:, 1, :], best_j[:, :], 15, None, ALU.bitwise_and))
                    link(V.tensor_copy(part_f[:, :, :], part_u[:, :, :]))
                    oh = onehot.rearrange("p (s r) -> p s r", s=TOPK)
                    for a in range(2):
                        link(V.tensor_tensor(oh, part_f[:, a, :].unsqueeze(2).to_broadcast([P, TOPK, TOPK]),
                                             iota16[:, :].unsqueeze(1).to_broadcast([P, TOPK, TOPK]), ALU.is_equal))
                        link(V.tensor_tensor(oh, oh, top_f[:, a, :].unsqueeze(1).to_broadcast([P, TOPK, TOPK]),
                                             ALU.mult))
                        link(V.tensor_reduce(pick[:, a, :], oh, AX, ALU.add))
                    link(V.tensor_scalar(pick[:, 0, :], pick[:, 0, :], float(NKEYS), float(l * NEXP),
                                         ALU.mult, ALU.add))
                    assert k[0] == CH
                    V.tensor_tensor(idx_u[b][:, :], pick[:, 0, :], pick[:, 1, :], ALU.add).then_inc(idx_ready, 1)
                    dve.wait_ge(gate_exp, g + (base + 1))
                    V.reciprocal(rbest[:, :], esumb[:, :]).then_inc(gate_r, 1)
                    dve.wait_ge(gate_r, g + (base + 1))
                    V.tensor_scalar(gate[:, b, :], ebest[:, :], rbest[:, 0:1], None, ALU.mult).then_inc(gate_done, 1)

                def weights_of(g, b):
                    dve.wait_ge(gelu_done, g + (base + 1))
                    dve.wait_ge(gate_done, g + (base + 1))
                    V.tensor_tensor(wgt[:, b, :], gel[:, b, :], gate[:, b, :], ALU.mult).then_inc(w_ready, 1)

                def accumulate(g, b):
                    dve.wait_ge(v_used, (g + base) * TOPK + TOPK)
                    tile = g // HEADS
                    for half in range(2):
                        dst = area_a[:, bass.ds(tile * D + half * 512, 512)]
                        ins = V.tensor_tensor(dst, dst, bank[2 * b + half][:, :], ALU.add)
                        ins.then_inc(acc_done, 1)
                    dve.wait_ge(acc_done, (g + (base + 1)) * 2)

                def dot(g, b, j):
                    dve.wait_ge(u_in[j % U_SLOTS], (g + base) * 32 + 16 * (j // U_SLOTS) + 16)
                    tile = g // HEADS
                    V.scalar_tensor_tensor(out=dot_junk, in0=u_rows[j % U_SLOTS], scalar=1.0,
                                           in1=y_flat[:, bass.ds(tile * D, D)], op0=ALU.mult, op1=ALU.mult,
                                           accum_out=dots[:, b, j:j + 1]).then_inc(dot_done, 1)
                    dve.wait_ge(dot_done, (g + base) * TOPK + j + 1)

                def step(g, b, first=False, second=False, last=False):
                    if not first:
                        weights_of(g - 1, 1 - b)
                        if not second:
                            accumulate(g - 2, b)
                    dve.wait_ge(idx_ready, g + (base + 1))
                    V.tensor_copy(idx_v[b][:, :], idx_u[b][:, :]).then_inc(idxv_ready, 1)
                    for j in range(TOPK // 2):
                        dot(g, b, j)
                    if not last:
                        top_k(g + 1, 1 - b)
                    for j in range(TOPK // 2, TOPK):
                        dot(g, b, j)

                top_k(0, 0)
                step(0, 0, first=True)
                step(1, 1, second=True)
                with dve.Fori(1, NH // 2 - 1) as i:
                    step(i * 2, 0)
                    step(i * 2 + 1, 1)
                step(NH - 2, 0)
                step(NH - 1, 1, last=True)
                weights_of(NH - 1, 1)
                accumulate(NH - 2, 0)
                accumulate(NH - 1, 1)
                counts[dve_c.name] = chain0 + NH * CH
                for s in range(S):
                    wait_taken(dve, ("bc5", l, s, 1))
                for t in range(T):
                    done(V.tensor_tensor(o_acc[:, t, :], o_acc[:, t, :], gate_bc[:, t // 2, :], ALU.mult))
                    done(V.tensor_tensor(x_res[:, t, :], x_res[:, t, :], o_acc[:, t, :], ALU.add),
                         peer_done if t == T - 1 else dve_c)
            mean_square(2)
            dve.wait_ge(fg_in, 16)
            for t in range(2):
                done(V.scalar_tensor_tensor(area_y[:, t, :], x_res[:, t, :], rstd[:, t:t + 1], final_g,
                                            ALU.mult, ALU.mult), out_ready)


def _tables():
    n = 2 * SEQ
    t = np.arange(SEQ)
    ang = 2.0 * np.pi * ((t[:, None] * t[None, :]) % n) / n
    cos, sin = np.cos(ang), -np.sin(ang)
    sin[:, 0] = 0.0
    alt = np.where(t % 2 == 0, 1.0, -1.0)
    cos_alt, sin_alt = cos.copy(), sin.copy()
    cos_alt[:, 0] = alt
    sin_alt[:, 0] = alt

    def tiles(a):
        return a.reshape(2, P, -1).transpose(1, 0, 2)

    f = np.float32
    tl = np.linspace(0.0, 1.0, SEQ, dtype=f)
    bands = np.linspace(1e-4, 15, 16, dtype=f)
    phase = (f(2.0 * math.pi / SEQ) * np.arange(SEQ, dtype=f)[:, None] * bands).astype(f)
    feat = np.concatenate([tl[:, None], np.cos(phase), -np.sin(phase)], axis=-1).astype(f)
    cols = np.zeros((P, 6), f)
    cols[:, 0:2] = -tl.reshape(2, P).T
    cols[:, 2:4] = 1.0
    cols[0, 2] = 0.0
    cols[:, 4:6] = 2.0 / n
    cols[0, 4] = 1.0 / n
    row, col = (t // GRID_W).astype(f), (t % GRID_W).astype(f)
    parts = []
    for dim in (64, 32):
        axis_dim = dim // 2
        inv = (f(10000.0) ** (-np.arange(0, axis_dim, 2, dtype=f) / f(axis_dim))).astype(f)
        angs = np.stack([row[:, None] * inv, col[:, None] * inv], axis=1)
        c, s = np.cos(angs), np.sin(angs)
        parts.append(np.stack([c, c], axis=2).reshape(SEQ, dim))
        parts.append(np.stack([-s, s], axis=2).reshape(SEQ, dim))
    mask = np.zeros((SEQ, 512), f)
    mask[:, 0:SEQ] = np.where(np.abs(t[:, None] - t[None, :]) <= 128, 0.0, -1e30)
    return {
        "k_ident": np.eye(P), "k_dft_c": tiles(cos), "k_dft_s": tiles(sin_alt), "k_dft_i": tiles(sin_alt.T),
        "k_dft_cn": tiles(cos_alt[:, 0:P]), "k_dft_s0": tiles(sin[:, 0:P]), "k_cols": cols, "k_feat": feat.T,
        "k_rope": tiles(np.concatenate(parts, axis=1)), "k_mask": tiles(mask),
        "k_iota": np.broadcast_to(np.arange(TOPK), (P, TOPK)), "k_zrows": np.zeros((LAYERS, 2, 2, HY_COLS)),
    }


def _lay_out(i):
    L = LAYERS

    def by_part(a):
        a = a.reshape(a.shape[:-1] + (-1, P))
        return np.moveaxis(a, -1, 0)

    same = ["x", "ctx", "w_mod", "hy_conv_w", "hy_conv_b", "hy_w3", "hy_bias", "wa_sink", "da_lq1",
            "da_lk1", "da_lq2", "da_lk2", "da_norm_g", "w_out", "peer_wq", "final_g"]
    out = {n: i[n] for n in same}
    out["c_cols"] = np.moveaxis(by_part(np.stack([i["c"][0], i["c_ctx"]])), 1, 2).reshape(P, KD * 2)
    w = i["w_in"].copy()
    q = i["w_in"][:, :, WA0:WA0 + 512].reshape(L, D, WA_KV, 4, 64)
    w[:, :, WA0:WA0 + 512] = q.transpose(0, 1, 3, 2, 4).reshape(L, D, 512)
    out["w_in"] = w
    out["b_mod"] = by_part(i["b_mod"])
    out["g12"] = by_part(np.stack([i["norm1_g"], i["norm2_g"]], axis=1))
    out["fcol"] = np.stack([i["hy_freq"], i["hy_b1"], i["hy_b2"]]).transpose(2, 1, 0)
    out["hy_w1"] = i["hy_w1"].transpose(1, 0, 2)
    out["hy_w2"] = i["hy_w2"].transpose(1, 0, 2)
    out["hy_decay"] = i["hy_decay"].reshape(L, -1)
    out["keysT"] = i["peer_keys"].transpose(0, 4, 1, 2, 3).reshape(L, P, 2 * HEADS, NKEYS)
    out["peer_u"] = i["peer_u"].reshape(L * NEXP, D)
    out["peer_v"] = i["peer_v"].reshape(L * NEXP, D)
    return out


def kernel(**inputs):
    import concourse.bacc as bacc
    from concourse.bass_utils import run_bass_kernel_spmd

    nc = bacc.Bacc("TRN2", target_bir_lowering=False, num_devices=1)
    arrays = {n: np.asarray(a) for n, a in inputs.items()}
    arrays = {n: np.ascontiguousarray(a) for n, a in _lay_out(arrays).items()}
    arrays.update({n: np.ascontiguousarray(a, dtype=np.float32) for n, a in _tables().items()})
    aps = {n: nc.dram_tensor(n, a.shape, F32, kind="ExternalInput").ap() for n, a in arrays.items()}
    out = nc.dram_tensor("out", (1, SEQ, D), F32, kind="ExternalOutput").ap()
    build(nc, aps, out)
    r = run_bass_kernel_spmd(nc, [arrays], core_ids=[0])
    return r.results[0]["out"]
```

```python
import math
from contextlib import ExitStack

import concourse.bass as bass
import numpy as np
from concourse import mybir

F32 = mybir.dt.float32
U32 = mybir.dt.uint32
ALU = mybir.AluOpType
ACT = mybir.ActivationFunctionType
AX = mybir.AxisListType.X

P = 128
D = 1024
KD = D // P
SEQ = 256
LAYERS = 2
GRID_W = 64
EPS = 1e-6
HYW = 256
HY_COLS = 3 * HYW
FW = 64
EMB = 33
IN_COLS = 2304
WA0 = HY_COLS
DA0 = 1536
WA_HEADS, WA_KV = 8, 2
WA_SCALE = 64 ** -0.5
DA_HEADS = 4
DA_SCALE = 32 ** -0.5
HEADS = 8
TOPK = 16
NKEYS = 128
NEXP = NKEYS * NKEYS
NMOD_CHUNKS = 48
LOW = -3.0e38
BANKS = 6
AHEAD = 3
SLOTS = 4
SLOT_W = 3072
U_SLOTS, V_SLOTS, G_SLOTS = 8, 4, 4
C1 = 6.28125
C2 = 2.0 * math.pi - C1
ROUND = 12582912.0
PI_IN = 3.1415925


def lam_init_of(layer):
    return 0.8 - 0.6 * math.exp(-0.3 * layer)


def q_tiles(layer):
    return 4 if layer < LAYERS - 1 else 2


def streams(layer):
    return q_tiles(layer) // 2


LOADS = []
for _l in range(LAYERS):
    LOADS += [("mod", _l, n) for n in range(16)]
    LOADS += [("in", _l, n) for n in range(6)]
    LOADS += [("out", _l, n) for n in range(4)]
    LOADS += [("q", _l, n) for n in range(8)]
LOAD_AT = {key: n for n, key in enumerate(LOADS)}


def proj_units(layer):
    return [(c, t) for c in range(6) for t in range(4 if (layer < LAYERS - 1 or c >= 3) else 2)]


def attention_maps(layer):
    out = []
    for t in range(q_tiles(layer)):
        out += [("wa", t, h, 0) for h in range(WA_HEADS)]
        out += [("da", t, h, m) for h in range(DA_HEADS) for m in range(2)]
    return out


def stat_column(kind, t, h, m):
    return t * WA_HEADS + h if kind == "wa" else 32 + (t * DA_HEADS + h) * 2 + m


def has_pv(unit):
    return unit[0] == "wa" or unit[3] == 1


GROUPS = []


def _group(key, engine):
    GROUPS.append((key, engine))


def _plan():
    flip = ("dve", "act")
    for l in range(LAYERS):
        _group(("flt1", l), "dve")
        for n in range(16):
            _group(("mod", l, n), "dve")
            if n == 1:
                _group(("flt2", l), "dve")
            if n == 3:
                for tt in range(2):
                    for o in range(2):
                        _group(("flt3", l, tt, o), "dve")
            if n == 8:
                for k in range(5):
                    _group(("spec", l, k), "act")
        _group(("col", l), "dve")
        for kk in range(KD):
            _group(("hT", l, kk), flip[kk % 2])
        for c, t in proj_units(l):
            _group(("pj", l, c, t), flip[t % 2])
        for b in range(9):
            _group(("tr", l, b), "act")
        for o in range(2):
            for m in range(2):
                _group(("re", l, o, m), "dve")
                _group(("im", l, o, m), "dve")
            for tt in range(2):
                _group(("inv", l, o, tt), "dve")
        maps = attention_maps(l)

        def score(n):
            _group(("s", l, n), "dve" if maps[n][0] == "wa" and maps[n][1] < 2 else "act")
        for n in range(AHEAD):
            score(n)
        for n, unit in enumerate(maps):
            if n + AHEAD < len(maps):
                score(n + AHEAD)
            if has_pv(unit):
                _group(("pt", l, n), "dve" if unit[0] == "wa" and n % 2 == 1 else "act")
        for kk in range(KD):
            _group(("yT", l, kk), flip[kk % 2])
        for t in range(q_tiles(l)):
            for n in range(4):
                _group(("wo", l, n, t), "dve")
            if t > 0:
                for half in range(2):
                    _group(("h2T", l, t - 1, half), "act")
        for half in range(2):
            _group(("h2T", l, q_tiles(l) - 1, half), "act")
        for hp in range(2 * HEADS + 1):
            if hp < 2 * HEADS:
                _group(("q", l, hp), "act")
            if hp > 0:
                _group(("sc", l, hp - 1), "dve")


_plan()
GROUP_AT = {key: n for n, (key, _) in enumerate(GROUPS)}
FREED_COUNT = []
_seen = {"dve": 0, "act": 0}
for _key, _engine in GROUPS:
    _seen[_engine] += 1
    FREED_COUNT.append(_seen[_engine])

LAST_USE = {}
for _l in range(LAYERS):
    for _n in range(16):
        LAST_USE["mod", _l, _n] = ("mod", _l, _n)
    for _n in range(6):
        LAST_USE["in", _l, _n] = ("pj", _l, _n, max(t for c, t in proj_units(_l) if c == _n))
    for _n in range(4):
        LAST_USE["out", _l, _n] = ("wo", _l, _n, q_tiles(_l) - 1)
    for _n in range(8):
        LAST_USE["q", _l, _n] = ("q", _l, 2 * _n + 1)

SQ_BEFORE = [l + sum(q_tiles(k) for k in range(l)) for l in range(LAYERS + 1)]
HEADS_BEFORE = [sum(HEADS * q_tiles(k) for k in range(l)) for l in range(LAYERS + 1)]


def build(nc, A, out):
    ctx = ExitStack()
    with ctx:
        def sb(name, shape, dt=F32):
            return ctx.enter_context(nc.sbuf_tensor("t_" + name, shape, dt))

        def sem(name):
            return ctx.enter_context(nc.semaphore(name))

        x_res = sb("x_res", [P, 4, D])
        area_h = sb("area_h", [P, 4096])
        area_p = sb("area_p", [P, 4 * IN_COLS])
        area_a = sb("area_a", [P, 4608])
        area_y = sb("area_y", [P, 4, D])
        ring = sb("ring", [P, SLOTS * SLOT_W])
        area_b = sb("area_b", [P, 6144])

        hT = area_h[:, :].rearrange("p (k t) -> p k t", k=KD)
        yre = area_h[:, 0:1024].rearrange("p (m n) -> p m n", m=2)
        yim = area_h[:, 1024:2048].rearrange("p (m n) -> p m n", m=2)
        z_buf = area_h[:, 2048:3072].rearrange("p (t s c) -> p t s c", t=2, s=2)
        hy_tmp = area_h[:, 3072:3584]
        hy_bias = area_h[:, 3584:4096].rearrange("p (o c) -> p o c", o=2)
        proj = area_p[:, :].rearrange("p (t c) -> p t c", t=4)
        junk = area_p[:, 0:D]
        scores = area_p[:, 0:4 * 2048]
        head_sc = area_p[:, 8192:8704].rearrange("p (b a k) -> p b a k", b=2, a=2)
        f_sum = area_a[:, 0:1024].rearrange("p (t n) -> p t n", t=2)
        f_dif = area_a[:, 1024:2048].rearrange("p (t n) -> p t n", t=2)
        f_win = area_a[:, 2048:3072]
        f_dec = area_a[:, 3072:4096]
        f_hw = area_a[:, 4096:4608]
        qkT = area_a[:, :].rearrange("p (b t) -> p b t", b=9)
        res_tmp = area_a[:, 0:256]
        qT = area_a[:, 0:1024].rearrange("p (b t) -> p b t", b=2)
        o_acc = area_a[:, 0:4096].rearrange("p (t n) -> p t n", t=4)
        diag = area_a[:, 4096:4608].rearrange("p (g n) -> p g n", g=G_SLOTS)
        w3_sb = area_y[0:FW, 0, :]
        f_arg = area_y[0:FW, 1, 0:256]
        f_rnd = area_y[0:FW, 1, 256:512]
        f_z1 = area_y[0:FW, 1, 512:768]
        f_z2 = area_y[0:FW, 1, 768:1024]
        conv_w = area_y[:, 0:3, :].rearrange("p a (b c) -> p (a b c)", b=1).rearrange("p (j c) -> p j c", j=4)
        u_prev = area_b[:, 0:3072].rearrange("p (t c) -> p t c", t=4)
        u_next = area_b[:, 3072:6144].rearrange("p (t c) -> p t c", t=4)
        p_buf = area_b[:, 0:512 * (AHEAD + 1)].rearrange("p (n k) -> p n k", n=AHEAD + 1)
        pT_buf = area_b[:, 2560:3584].rearrange("p (n k) -> p n k", n=2)
        rope_1 = area_a[:, 0:640]
        rope_2 = area_a[:, 640:1280]
        mod_rows = area_b[0:2, :]
        bmod_rows = area_p[0:2, 1024:7168]
        g2_rows = area_p[0:2, 7168:8192]
        da_sq = area_b[:, 4352:5376].rearrange("p (t c) -> p t c", t=4)
        gate_bc = area_b[:, 0:2048].rearrange("p (s n) -> p s n", s=2)
        a2_bc = area_b[:, 2048:4096].rearrange("p (s n) -> p s n", s=2)
        b2_bc = area_b[:, 4096:6144].rearrange("p (s n) -> p s n", s=2)
        keysT = area_b[:, 2048:4096].rearrange("p (h k) -> p h k", h=16)
        dot_junk = area_b[:, 4096:4608].bitcast(mybir.dt.bfloat16)
        cand = area_b[:, 5120:5376]
        cand2 = area_b[:, 5376:5632]
        onehot = area_b[:, 5632:5888]
        sc_left = area_b[:, 5888:6144].rearrange("p (a k) -> p a k", a=2)
        final_g = area_b[:, 2048:3072]

        y_flat = area_y[:, :, :].rearrange("p t n -> p (t n)")

        def wslot(key):
            s = LOAD_AT[key] % SLOTS
            return ring[:, s * SLOT_W:(s + 1) * SLOT_W]

        u_rows = [ring[:, n * D:(n + 1) * D] for n in range(U_SLOTS)]
        v_rows = [ring[:, (U_SLOTS + n) * D:(U_SLOTS + n + 1) * D] for n in range(V_SLOTS)]

        ident = sb("ident", [P, P])
        dft_c = sb("dft_c", [P, 2, 256])
        dft_s = sb("dft_s", [P, 2, 256])
        dft_i = sb("dft_i", [P, 2, 256])
        dft_cn = sb("dft_cn", [P, 2, P])
        dft_s0 = sb("dft_s0", [P, 2, P])
        cols = sb("cols", [P, 6])
        feat = sb("feat", [EMB, 256])
        rope = sb("rope", [P, 2, 192])
        mask = sb("mask", [P, 2, 512])
        iota16 = sb("iota16", [P, TOPK])
        c_raw = sb("c_raw", [P, KD * 2])
        c_tmp = sb("c_tmp", [P, KD * 2])
        c_act = sb("c_act", [P, KD, 2])
        g1 = sb("g1", [P, LAYERS, KD])
        sinks = sb("sinks", [P, LAYERS, WA_HEADS])
        nsinks = sb("nsinks", [P, LAYERS, WA_HEADS])
        lam_v = sb("lam_v", [P, 4, LAYERS * 32])
        lam_p = sb("lam_p", [P, 2, LAYERS * 32])
        lam_s = sb("lam_s", [P, 2, LAYERS])
        lam_n = sb("lam_n", [P, LAYERS])
        dag = sb("dag", [P, LAYERS, 64])
        fcol = sb("fcol", [FW, LAYERS, 3])
        w1_sb = sb("w1_sb", [EMB, LAYERS, FW])
        w2_sb = sb("w2_sb", [FW, LAYERS, FW])
        spec = sb("spec", [P, 5, 512])
        modc = sb("modc", [P, 2 * KD, 2])
        a1 = sb("a1", [P, KD, 2])
        ss = sb("ss", [P, 4])
        ms = sb("ms", [P, 4])
        rstd = sb("rstd", [P, 4])
        mhalf = sb("mhalf", [P, 16])
        mx = sb("mx", [P, 64])
        nm = sb("nm", [P, 64])
        lsum = sb("lsum", [P, 64])
        esink = sb("esink", [P, 4, WA_HEADS])
        esum = sb("esum", [P, 4, WA_HEADS])
        rr = sb("rr", [P, 2])
        da_ss = sb("da_ss", [P, 4, DA_HEADS])
        da_ms = sb("da_ms", [P, 4, DA_HEADS])
        da_r = sb("da_r", [P, 4, DA_HEADS])
        da_r0 = sb("da_r0", [P, 2 * DA_HEADS])
        top_s = sb("top_s", [P, 2, TOPK])
        top_i = sb("top_i", [P, 2, TOPK], U32)
        top_f = sb("top_f", [P, 2, TOPK])
        best_s = sb("best_s", [P, TOPK])
        best_j = sb("best_j", [P, TOPK], U32)
        part_u = sb("part_u", [P, 2, TOPK], U32)
        part_f = sb("part_f", [P, 2, TOPK])
        pick = sb("pick", [P, 2, TOPK])
        nbest = sb("nbest", [P, 1])
        ebest = sb("ebest", [P, TOPK])
        esumb = sb("esumb", [P, 1])
        rbest = sb("rbest", [P, 1])
        gate = sb("gate", [P, 2, TOPK])
        idx_u = [sb(f"idx_u{b}", [P, TOPK], U32) for b in range(2)]
        idx_v = [sb(f"idx_v{b}", [P, TOPK], U32) for b in range(2)]
        dots = sb("dots", [P, 2, TOPK])
        gel = sb("gel", [P, 2, TOPK])
        wgt = sb("wgt", [P, 2, TOPK])

        bank = [ctx.enter_context(nc.psum_tensor(f"bank{b}", [P, 512], F32)) for b in range(8)]
        mod_scr = nc.dram_tensor("mod_scr", (LAYERS, 2, 6 * D), F32, kind="Internal").ap()
        u_scr = nc.dram_tensor("u_scr", (LAYERS, 2, SEQ + 2, HY_COLS), F32, kind="Internal").ap()

        pe_group = sem("pe_group")
        dve_freed = sem("dve_freed")
        act_freed = sem("act_freed")
        consts_in = sem("consts_in")
        w_in_slot = [sem(f"w_in_slot{n}") for n in range(SLOTS)]
        w3_in = sem("w3_in")
        convw_in = sem("convw_in")
        hybias_in = sem("hybias_in")
        keys_in = sem("keys_in")
        fg_in = sem("fg_in")
        zrow_out = sem("zrow_out")
        u_out = sem("u_out")
        u_back = sem("u_back")
        dve_c = sem("dve_c")
        act_c = sem("act_c")
        pool_c = sem("pool_c")
        c_ready = sem("c_ready")
        c_exp = sem("c_exp")
        sin_arg = sem("sin_arg")
        sin_done = sem("sin_done")
        win_arg = sem("win_arg")
        win_done = sem("win_done")
        fsum_ready = sem("fsum_ready")
        lam_sum = sem("lam_sum")
        lam_exp = sem("lam_exp")
        bmod_in = sem("bmod_in")
        rows_ready = sem("rows_ready")
        rows_out = sem("rows_out")
        rows_in = sem("rows_in")
        gate5_in = sem("gate5_in")
        mod_ready = sem("mod_ready")
        sq_ready = sem("sq_ready")
        ms_ready = sem("ms_ready")
        rstd_ready = sem("rstd_ready")
        xn_ready = sem("xn_ready")
        uprev_ready = sem("uprev_ready")
        conv_done = sem("conv_done")
        roped = sem("roped")
        y_spec = sem("y_spec")
        z_ready = sem("z_ready")
        neg_max = sem("neg_max")
        exp_done = sem("exp_done")
        comb_done = sem("comb_done")
        pv_done = sem("pv_done")
        o_taken = sem("o_taken")
        sink_arg = sem("sink_arg")
        sink_exp = sem("sink_exp")
        y_ready = sem("y_ready")
        x_done = sem("x_done")
        h2_ready = sem("h2_ready")
        sc_in = sem("sc_in")
        best_ready = sem("best_ready")
        gate_exp = sem("gate_exp")
        idx_ready = sem("idx_ready")
        idxv_ready = sem("idxv_ready")
        u_in = [sem(f"u_in{n}") for n in range(U_SLOTS)]
        v_in = [sem(f"v_in{n}") for n in range(V_SLOTS)]
        dot_done = sem("dot_done")
        gelu_done = sem("gelu_done")
        w_ready = sem("w_ready")
        diag_ready = sem("diag_ready")
        v_used = sem("v_used")
        acc_done = sem("acc_done")
        acc_zero = sem("acc_zero")
        gate_r = sem("gate_r")
        gate_done = sem("gate_done")
        peer_done = sem("peer_done")
        out_ready = sem("out_ready")
        out_sent = sem("out_sent")

        freed_sem = {"dve": dve_freed, "act": act_freed}

        def wait_group(eng, key):
            eng.wait_ge(pe_group, GROUP_AT[key] + 1)

        def wait_taken(eng, key):
            n = GROUP_AT[key]
            eng.wait_ge(freed_sem[GROUPS[n][1]], FREED_COUNT[n])

        def stand_alone(eng):
            eng.nop(nofuse=True)

        def at(key):
            return bank[GROUP_AT[key] % BANKS]

        const_list = [
            (ident[:, :], A["k_ident"]), (dft_c[:, :, :], A["k_dft_c"]), (dft_s[:, :, :], A["k_dft_s"]),
            (dft_i[:, :, :], A["k_dft_i"]), (dft_cn[:, :, :], A["k_dft_cn"]), (dft_s0[:, :, :], A["k_dft_s0"]),
            (cols[:, :], A["k_cols"]), (feat[:, :], A["k_feat"]), (rope[:, :, :], A["k_rope"]),
            (mask[:, :, :], A["k_mask"]), (iota16[:, :], A["k_iota"]),
            (c_raw[:, :], A["c_cols"]), (g1[:, :, :], A["g1"]),
            (sinks[:, :, :], A["wa_sink"].unsqueeze(0).to_broadcast([P, LAYERS, WA_HEADS])),
            (dag[:, :, :], A["da_norm_g"].unsqueeze(0).to_broadcast([P, LAYERS, 64])),
            (fcol[:, :, :], A["fcol"]), (w1_sb[:, :, :], A["hy_w1"]), (w2_sb[:, :, :], A["hy_w2"]),
        ]
        for n, name in enumerate(("da_lq1", "da_lk1", "da_lq2", "da_lk2")):
            const_list.append((lam_v[:, n, :], A[name].rearrange("l d -> (l d)").unsqueeze(0)
                               .to_broadcast([P, LAYERS * 32])))
        for t in range(4):
            src = A["x"] if t < 2 else A["ctx"]
            const_list.append((x_res[:, t, :], src[0, (t % 2) * P:(t % 2 + 1) * P, :]))
        CONSTS = 16 * len(const_list)

        block = ctx.enter_context(nc.Block())

        @block.sync
        def _(sp):
            for dst, src in const_list:
                sp.dma_start(dst, src).then_inc(consts_in, 16)
            sp.dma_start(u_scr[:, :, 0:SEQ + 2:SEQ + 1, :], A["k_zrows"]).then_inc(zrow_out, 16)

            def load_weights(kind, l, n):
                at_n = LOAD_AT[kind, l, n]
                if at_n >= SLOTS:
                    wait_group(sp, LAST_USE[LOADS[at_n - SLOTS]])
                if kind == "mod" and l > 0 and n == 0:
                    sp.wait_ge(dot_done, TOPK * HEADS_BEFORE[l])
                    sp.wait_ge(v_used, TOPK * HEADS_BEFORE[l])
                src, width = {"mod": (A["w_mod"], 384), "in": (A["w_in"], 384),
                              "out": (A["w_out"], 256), "q": (A["peer_wq"], 256)}[kind]
                dst = wslot((kind, l, n))[:, 0:KD * width].rearrange("p (k c) -> p k c", k=KD)
                sp.dma_start(dst, src[l].rearrange("(k p) c -> p k c", p=P)[:, :, n * width:(n + 1) * width]) \
                    .then_inc(w_in_slot[at_n % SLOTS], 16)

            for l in range(LAYERS):
                if l > 0:
                    sp.wait_ge(peer_done, l)
                sp.dma_start(w3_sb, A["hy_w3"][l]).then_inc(w3_in, 16)
                sp.dma_start(f_dec, A["hy_decay"][l].unsqueeze(0).to_broadcast([P, 1024])).then_inc(w3_in, 16)
                sp.dma_start(bmod_rows, A["b_mod"][l:l + 1, :].to_broadcast([2, 6 * D])).then_inc(bmod_in, 16)
                sp.dma_start(g2_rows, A["norm2_g"][l:l + 1, :].to_broadcast([2, D])).then_inc(bmod_in, 16)
                for n in range(16):
                    load_weights("mod", l, n)
                for n in range(4):
                    load_weights("in", l, n)
                sp.wait_ge(rows_ready, l + 1)
                sp.dma_start(mod_scr[l], mod_rows).then_inc(rows_out, 16)
                wait_group(sp, ("hT", l, KD - 1))
                for j in range(3):
                    sp.dma_start(conv_w[:, j, :], A["hy_conv_w"][l, j:j + 1, :].to_broadcast([P, HY_COLS])) \
                        .then_inc(convw_in, 16)
                sp.dma_start(conv_w[:, 3, :], A["hy_conv_b"][l:l + 1, :].to_broadcast([P, HY_COLS])) \
                    .then_inc(convw_in, 16)
                for c in range(2):
                    for t in range(q_tiles(l)):
                        wait_taken(sp, ("pj", l, c, t))
                for t in range(q_tiles(l)):
                    sp.dma_start(u_scr[l, t // 2, 1 + (t % 2) * P:1 + (t % 2 + 1) * P, :],
                                 proj[:, t, 0:HY_COLS]).then_inc(u_out, 16)
                if l == 0:
                    sp.wait_ge(zrow_out, 16)
                sp.wait_ge(rows_out, 16 * (l + 1))
                sp.wait_ge(u_out, 16 * sum(q_tiles(k) for k in range(l + 1)))
                for t in range(q_tiles(l)):
                    r = (t % 2) * P
                    sp.dma_start(u_prev[:, t, :], u_scr[l, t // 2, r:r + P, :]).then_inc(u_back, 16)
                    sp.dma_start(u_next[:, t, :], u_scr[l, t // 2, r + 2:r + 2 + P, :]).then_inc(u_back, 16)
                for n in range(4, 6):
                    load_weights("in", l, n)
                wait_group(sp, ("pj", l) + proj_units(l)[-1])
                sp.dma_start(hy_bias, A["hy_bias"][l].unsqueeze(0).to_broadcast([P, 2, HYW])).then_inc(hybias_in, 16)
                for n in range(4):
                    load_weights("out", l, n)
                sp.wait_ge(y_ready, sum(q_tiles(k) for k in range(l + 1)))
                for s in range(streams(l)):
                    for dst, v in ((gate_bc, 2), (a2_bc, 4), (b2_bc, 3)):
                        sp.dma_start(dst[:, s, :], mod_scr[l, s:s + 1, v * D:(v + 1) * D].to_broadcast([P, D])) \
                            .then_inc(rows_in, 16)
                for n in range(4):
                    load_weights("q", l, n)
                sp.wait_ge(h2_ready, sum(q_tiles(k) for k in range(l + 1)))
                for s in range(streams(l)):
                    sp.dma_start(gate_bc[:, s, :], mod_scr[l, s:s + 1, 5 * D:6 * D].to_broadcast([P, D])) \
                        .then_inc(gate5_in, 16)
                sp.dma_start(keysT, A["keysT"][l]).then_inc(keys_in, 16)
                for n in range(4, 8):
                    load_weights("q", l, n)
                if l == LAYERS - 1:
                    wait_group(sp, ("sc", l, 2 * HEADS - 1))
                    sp.dma_start(final_g, A["final_g"].unsqueeze(0).to_broadcast([P, D])).then_inc(fg_in, 16)
            for t in range(2):
                sp.wait_ge(out_ready, t + 1)
                sp.dma_start(out[0, t * P:(t + 1) * P, :], area_y[:, t, :]).then_inc(out_sent, 16)
            sp.wait_ge(out_sent, 32)

        @block.tensor
        def _(pe):
            def open_group(key):
                n = GROUP_AT[key]
                if n >= BANKS:
                    pe.wait_ge(freed_sem[GROUPS[n - BANKS][1]], FREED_COUNT[n - BANKS])
                return bank[n % BANKS]

            def close(ins):
                ins.then_inc(pe_group, 1)

            def weights(kind, l, n, width):
                k = LOAD_AT[kind, l, n]
                pe.wait_ge(w_in_slot[k % SLOTS], 16 * (k // SLOTS + 1))
                return wslot((kind, l, n))[:, 0:KD * width].rearrange("p (k c) -> p k c", k=KD)

            def transposes(key, blocks):
                ps = open_group(key)
                for n, src in enumerate(blocks):
                    last = nc.tensor.transpose(ps[:, n * P:(n + 1) * P], src, ident[:, :])
                close(last)

            pe.wait_ge(consts_in, CONSTS)
            o_count = 0
            for l in range(LAYERS):
                T, S = q_tiles(l), streams(l)
                ps = open_group(("flt1", l))
                close(nc.tensor.matmul(ps[0:FW, 0:256], w1_sb[:, l, :], feat[:, :], start=True, stop=True))
                pe.wait_ge(c_ready, 1)
                for n in range(16):
                    w = weights("mod", l, n, 384)
                    ps = open_group(("mod", l, n))
                    for kk in range(KD):
                        last = nc.tensor.matmul(ps[0:2, 0:384], c_act[:, kk, :], w[:, kk, :],
                                                start=kk == 0, stop=kk == KD - 1)
                    close(last)
                    if n == 1:
                        pe.wait_ge(sin_done, 2 * l + 1)
                        ps = open_group(("flt2", l))
                        close(nc.tensor.matmul(ps[0:FW, 0:256], w2_sb[:, l, :], f_z1, start=True, stop=True))
                    if n == 3:
                        pe.wait_ge(sin_done, 2 * l + 2)
                        pe.wait_ge(w3_in, 32 * (l + 1))
                        for tt in range(2):
                            for o in range(2):
                                ps = open_group(("flt3", l, tt, o))
                                close(nc.tensor.matmul(ps[:, :], f_z2[:, tt * P:(tt + 1) * P],
                                                       w3_sb[:, o * 512:(o + 1) * 512], start=True, stop=True))
                    if n == 8:
                        pe.wait_ge(fsum_ready, 4 * (l + 1))
                        for k in range(5):
                            ps = open_group(("spec", l, k))
                            mat = [dft_c[:, :, 0:P], dft_c[:, :, P:256], dft_s0[:, :, :], dft_s[:, :, P:256],
                                   dft_cn[:, :, :]][k]
                            rhs = f_dif if k in (2, 3) else f_sum
                            for tt in range(2):
                                last = nc.tensor.matmul(ps[:, :], mat[:, tt, :], rhs[:, tt, :],
                                                        start=tt == 0, stop=tt == 1)
                            close(last)
                wait_taken(pe, ("mod", l, 15))
                ps = open_group(("col", l))
                for k in range(2 * KD):
                    last = nc.tensor.transpose(ps[:, 2 * k:2 * k + 2], mod_rows[:, k * P:(k + 1) * P],
                                               ident[0:2, 0:2])
                close(last)
                pe.wait_ge(xn_ready, 4 * (l + 1))
                for kk in range(KD):
                    transposes(("hT", l, kk), [area_y[:, t, kk * P:(kk + 1) * P] for t in range(4)])
                for kk in range(KD - 2, KD):
                    wait_taken(pe, ("hT", l, kk))
                for c, t in proj_units(l):
                    w = weights("in", l, c, 384)
                    ps = open_group(("pj", l, c, t))
                    for kk in range(KD):
                        last = nc.tensor.matmul(ps[:, 0:384], hT[:, kk, t * P:(t + 1) * P], w[:, kk, :],
                                                start=kk == 0, stop=kk == KD - 1)
                    close(last)
                pe.wait_ge(roped, 4 * (l + 1))
                for t in range(2, 4):
                    for c in range(2, 6):
                        if (c, t) in proj_units(l):
                            wait_taken(pe, ("pj", l, c, t))
                for b in range(9):
                    tiles = range(4) if b in (4, 7, 8) else range(T)
                    blocks = []
                    for t in tiles:
                        if b < 4:
                            src = proj[:, t, WA0 + b * P:WA0 + (b + 1) * P]
                        elif b == 4:
                            src = proj[:, t, WA0 + 512:WA0 + 640]
                        else:
                            src = proj[:, t, DA0 + (b - 5) * P:DA0 + (b - 4) * P]
                        blocks.append(src)
                    transposes(("tr", l, b), blocks)
                pe.wait_ge(conv_done, l + 1)
                for o in range(2):
                    if o == 1:
                        pe.wait_ge(z_ready, 2 * (l + 1))
                    for m in range(2):
                        for name, mat in (("re", dft_c), ("im", dft_s)):
                            ps = open_group((name, l, o, m))
                            for tt in range(2):
                                if o == 0:
                                    z = area_p[:, :].rearrange("p (s t c) -> p s t c", s=2, t=2)[:, 0:S, tt, 512:768]
                                else:
                                    z = z_buf[:, tt, 0:S, :]
                                last = nc.tensor.matmul(ps[:, 0:S * HYW], mat[:, tt, m * P:(m + 1) * P], z,
                                                        start=tt == 0, stop=tt == 1)
                            close(last)
                    pe.wait_ge(y_spec, 4 * l + 2 * o + 2)
                    for tt in range(2):
                        ps = open_group(("inv", l, o, tt))
                        for m in range(2):
                            for mat, y in ((dft_c, yre), (dft_i, yim)):
                                last = nc.tensor.matmul(ps[:, 0:S * HYW], mat[:, m, tt * P:(tt + 1) * P],
                                                        y[:, m, 0:S * HYW], start=(m == 0 and mat is dft_c),
                                                        stop=(m == 1 and mat is dft_i))
                        close(last)
                maps = attention_maps(l)
                maps_before = sum(len(attention_maps(k)) for k in range(l))
                combs_before = sum(DA_HEADS * q_tiles(k) for k in range(l))
                wait_taken(pe, ("tr", l, 8))

                def score(n):
                    kind, t, h, m = maps[n]
                    ps = open_group(("s", l, n))
                    keys = slice(0, 512) if t < 2 else slice(256, 512)
                    width = keys.stop - keys.start
                    if kind == "wa":
                        r, b, kb = 64 * (h // 4), h % 4, 4
                        rows = slice(r, r + 64)
                    else:
                        hm = 2 * h + m
                        r, b, kb = 32 * (hm % 4), 5 + hm // 4, 7 + hm // 4
                        rows = slice(r, r + 32)
                    close(nc.tensor.matmul(ps[:, 0:width], qkT[rows, b, t * P:(t + 1) * P], qkT[rows, kb, keys],
                                           start=True, stop=True))

                def transpose_probs(n, combs):
                    kind, t, h, m = maps[n]
                    if kind == "wa":
                        pe.wait_ge(exp_done, maps_before + n + 1)
                    else:
                        pe.wait_ge(comb_done, combs_before + combs)
                    transposes(("pt", l, n), [p_buf[:, n % (AHEAD + 1), c * P:(c + 1) * P] for c in range(4 if t < 2 else 2)])

                def times_values(n, e):
                    nonlocal o_count
                    kind, t, h, m = maps[n]
                    wait_taken(pe, ("pt", l, n))
                    if h == 0:
                        o_count += 1
                        if o_count > 2:
                            pe.wait_ge(o_taken, o_count - 2)
                    ob = bank[BANKS + (o_count - 1) % 2]
                    col = WA0 + 640 + 64 * (h // 4) if kind == "wa" else DA0 + 512 + 64 * h
                    chunks = list(range(4)) if t < 2 else [2, 3]
                    for i, c in enumerate(chunks):
                        last = nc.tensor.matmul(ob[:, h * 64:(h + 1) * 64], pT_buf[:, e % 2, i * P:(i + 1) * P],
                                                proj[:, c, col:col + 64], start=i == 0, stop=i == len(chunks) - 1)
                    if h == (WA_HEADS if kind == "wa" else DA_HEADS) - 1:
                        last.then_inc(pv_done, 1)

                for n in range(AHEAD):
                    score(n)
                events = []
                combs = 0
                for n, unit in enumerate(maps):
                    if n + AHEAD < len(maps):
                        score(n + AHEAD)
                    if has_pv(unit):
                        if unit[0] == "da":
                            combs += 1
                        transpose_probs(n, combs)
                        events.append(n)
                        if len(events) > 1:
                            times_values(events[-2], len(events) - 2)
                times_values(events[-1], len(events) - 1)
                pe.wait_ge(y_ready, sum(q_tiles(k) for k in range(l + 1)))
                for kk in range(KD):
                    transposes(("yT", l, kk), [area_y[:, t, kk * P:(kk + 1) * P] for t in range(T)])
                for kk in range(KD - 2, KD):
                    wait_taken(pe, ("yT", l, kk))
                tiles_before = sum(q_tiles(k) for k in range(l))

                def transpose_h2(t):
                    pe.wait_ge(h2_ready, tiles_before + t + 1)
                    for half in range(2):
                        transposes(("h2T", l, t, half),
                                   [area_y[:, t, (half * 4 + j) * P:(half * 4 + j + 1) * P] for j in range(4)])

                for t in range(T):
                    for n in range(4):
                        w = weights("out", l, n, 256)
                        ps = open_group(("wo", l, n, t))
                        for kk in range(KD):
                            last = nc.tensor.matmul(ps[:, 0:256], hT[:, kk, t * P:(t + 1) * P], w[:, kk, :],
                                                    start=kk == 0, stop=kk == KD - 1)
                        close(last)
                    if t > 0:
                        transpose_h2(t - 1)
                transpose_h2(T - 1)
                wait_taken(pe, ("h2T", l, T - 1, 1))
                pe.wait_ge(keys_in, 16 * (l + 1))
                for hp in range(2 * HEADS + 1):
                    if hp < 2 * HEADS:
                        w = weights("q", l, hp // 2, 256)
                        c = (hp % 2) * P
                        ps = open_group(("q", l, hp))
                        for kk in range(KD):
                            last = nc.tensor.matmul(ps[:, 0:T * P], w[:, kk, c:c + P], hT[:, kk, 0:T * P],
                                                    start=kk == 0, stop=kk == KD - 1)
                        close(last)
                    if hp > 0:
                        wait_taken(pe, ("q", l, hp - 1))
                        ps = open_group(("sc", l, hp - 1))
                        for t in range(T):
                            last = nc.tensor.matmul(ps[:, t * P:(t + 1) * P],
                                                    qT[:, (hp - 1) % 2, t * P:(t + 1) * P], keysT[:, hp - 1, :],
                                                    start=True, stop=True)
                        close(last)

                base = HEADS_BEFORE[l]
                NH = HEADS * T

                def v_head(g, b, first):
                    if not first:
                        pe.wait_ge(acc_done, (g + (base - 1)) * 2)
                    for j in range(TOPK):
                        pe.wait_ge(v_in[j % V_SLOTS], (g + base) * (16 * TOPK // V_SLOTS) + 16 * (j // V_SLOTS) + 16)
                        pe.wait_ge(diag_ready, (g + base) * TOPK + j + 1)
                        for half in range(2):
                            last = nc.tensor.matmul(bank[2 * b + half][:, :], diag[:, j % G_SLOTS, :],
                                                    v_rows[j % V_SLOTS][:, half * 512:(half + 1) * 512],
                                                    start=j == 0, stop=j == TOPK - 1)
                        last.then_inc(v_used, 1)

                wait_taken(pe, ("sc", l, 2 * HEADS - 1))
                v_head(0, 0, True)
                v_head(1, 1, True)
                with pe.Fori(1, NH // 2 - 1) as i:
                    v_head(i * 2, 0, False)
                    v_head(i * 2 + 1, 1, False)
                v_head(NH - 2, 0, False)
                v_head(NH - 1, 1, False)
                pe.wait_ge(acc_done, 2 * (base + NH))

        @block.scalar
        def _(act):
            chained = [0]

            def chain(ins):
                chained[0] += 1
                ins.then_inc(act_c, 1)
                act.wait_ge(act_c, chained[0])

            def freed(ins):
                ins.then_inc(act_freed, 1)

            act.wait_ge(consts_in, CONSTS)
            nc.scalar.activation(c_tmp[:, :], c_raw[:, :], ACT.Exp, scale=-1.0).then_inc(c_exp, 1)
            act.wait_ge(lam_sum, 1)
            nc.scalar.activation(lam_s[:, :, :], lam_s[:, :, :], ACT.Exp).then_inc(lam_exp, 1)
            for l in range(LAYERS):
                T, S = q_tiles(l), streams(l)
                for n, z in enumerate((f_z1, f_z2)):
                    act.wait_ge(sin_arg, 2 * l + n + 1)
                    nc.scalar.activation(z, f_arg, ACT.Sin).then_inc(sin_done, 1)
                act.wait_ge(win_arg, l + 1)
                for tt in range(2):
                    if tt:
                        act.wait_ge(fsum_ready, 4 * l + 2)
                    nc.scalar.activation(f_win, f_dec, ACT.Exp, scale=cols[:, tt:tt + 1]).then_inc(win_done, 1)
                for n in range(5):
                    wait_group(act, ("spec", l, n))
                    scale = cols[:, 4:5] if n in (0, 2, 4) else cols[:, 5:6]
                    freed(nc.scalar.activation(spec[:, n, :], at(("spec", l, n))[:, :], ACT.Copy, scale=scale))
                if l > 0:
                    act.wait_ge(peer_done, l)
                for t in range(4):
                    ins = nc.scalar.activation(junk, x_res[:, t, :], ACT.Square, accum_out=ss[:, t:t + 1])
                    if t < 3:
                        chain(ins)
                ins.then_inc(sq_ready, 1)
                act.wait_ge(mod_ready, l + 1)
                for kk in range(1, KD, 2):
                    wait_group(act, ("hT", l, kk))
                    for s in range(2):
                        ins = nc.scalar.activation(hT[:, kk, s * 256:(s + 1) * 256],
                                                   at(("hT", l, kk))[:, s * 256:(s + 1) * 256], ACT.Identity,
                                                   bias=modc[:, kk, s:s + 1], scale=a1[:, kk, s:s + 1])
                    freed(ins)
                for c, t in proj_units(l):
                    if t % 2 == 1:
                        wait_group(act, ("pj", l, c, t))
                        freed(nc.scalar.activation(proj[:, t, c * 384:(c + 1) * 384],
                                                   at(("pj", l, c, t))[:, 0:384], ACT.Copy))
                for b in range(9):
                    wait_group(act, ("tr", l, b))
                    width = 512 if b in (4, 7, 8) else T * P
                    freed(nc.scalar.activation(qkT[:, b, 0:width], at(("tr", l, b))[:, 0:width], ACT.Copy))
                maps = attention_maps(l)
                maps_before = sum(len(attention_maps(k)) for k in range(l))

                def exps(n):
                    kind, t, h, m = maps[n]
                    c = stat_column(*maps[n])
                    act.wait_ge(neg_max, maps_before + n + 1)
                    width = 512 if t < 2 else 256
                    masked = kind == "wa" and t < 2
                    src = p_buf[:, n % (AHEAD + 1), 0:width] if masked else at(("s", l, n))[:, 0:width]
                    if not masked:
                        wait_group(act, ("s", l, n))
                    ins = nc.scalar.activation(p_buf[:, n % (AHEAD + 1), 0:width], src, ACT.Exp, bias=nm[:, c:c + 1],
                                               scale=WA_SCALE if kind == "wa" else DA_SCALE,
                                               accum_out=lsum[:, c:c + 1])
                    ins.then_inc(exp_done, 1)
                    if not masked:
                        act.wait_ge(exp_done, maps_before + n + 1)
                        act.sem_inc(act_freed, 1)

                tiles_before = sum(q_tiles(k) for k in range(l))
                for n in range(AHEAD - 1):
                    exps(n)
                e = 0
                for n, unit in enumerate(maps):
                    if n + AHEAD - 1 < len(maps):
                        exps(n + AHEAD - 1)
                    if has_pv(unit):
                        if GROUPS[GROUP_AT["pt", l, n]][1] == "act":
                            wait_group(act, ("pt", l, n))
                            width = 512 if unit[1] < 2 else 256
                            freed(nc.scalar.activation(pT_buf[:, e % 2, 0:width],
                                                       at(("pt", l, n))[:, 0:width], ACT.Copy))
                        e += 1
                    if unit[0] == "da" and unit[2:] == (DA_HEADS - 1, 1):
                        t = unit[1]
                        act.wait_ge(sink_arg, tiles_before + t + 1)
                        nc.scalar.activation(esink[:, t, :], esink[:, t, :], ACT.Exp).then_inc(sink_exp, 1)
                for kk in range(1, KD, 2):
                    wait_group(act, ("yT", l, kk))
                    freed(nc.scalar.activation(hT[:, kk, 0:T * P], at(("yT", l, kk))[:, 0:T * P], ACT.Copy))
                def take_h2T(t):
                    for half in range(2):
                        key = ("h2T", l, t, half)
                        wait_group(act, key)
                        freed(nc.scalar.activation(hT[:, half * 4:half * 4 + 4, t * P:(t + 1) * P],
                                                   at(key)[:, :].rearrange("p (k c) -> p k c", k=4), ACT.Copy))

                tiles_before = sum(q_tiles(k) for k in range(l))
                for t in range(T):
                    act.wait_ge(x_done, tiles_before + t + 1)
                    nc.scalar.activation(junk, x_res[:, t, :], ACT.Square, accum_out=ss[:, t:t + 1]) \
                        .then_inc(sq_ready, 1)
                    act.wait_ge(sq_ready, SQ_BEFORE[l] + 1 + t + 1)
                    if t > 0:
                        take_h2T(t - 1)
                take_h2T(T - 1)
                base = HEADS_BEFORE[l]
                NH = HEADS * T

                def copy_scores(g, b):
                    act.wait_ge(idx_ready, g + (base - 1))
                    nc.scalar.activation(head_sc[:, b, :, :].rearrange("p a k -> p (a k)"),
                                         scores[:, bass.ds(g * 256, 256)], ACT.Copy).then_inc(sc_in, 1)

                def gate_exps(g):
                    act.wait_ge(best_ready, g + (base + 1))
                    nc.scalar.activation(ebest[:, :], best_s[:, :], ACT.Exp, bias=nbest[:, 0:1],
                                         accum_out=esumb[:, 0:1]).then_inc(gate_exp, 1)

                def gelu(g, b):
                    act.wait_ge(dot_done, (g + base) * TOPK + TOPK)
                    nc.scalar.activation(gel[:, b, :], dots[:, b, :], ACT.Gelu).then_inc(gelu_done, 1)

                def diagonals(g, b, js, first=False):
                    act.wait_ge(w_ready, g + (base + 1))
                    for j in js:
                        if not (first and base == 0 and j < G_SLOTS):
                            act.wait_ge(v_used, (g + base) * TOPK + j - G_SLOTS + 1)
                        nc.scalar.activation(diag[:, j % G_SLOTS, :], ident[:, :], ACT.Copy,
                                             scale=wgt[:, b, j:j + 1]).then_inc(diag_ready, 1)

                def step(g, b, first=False, last=False):
                    if not last:
                        copy_scores(g + 1, 1 - b)
                    diagonals(g - 1, 1 - b, range(TOPK // 2), first)
                    if not last:
                        gate_exps(g + 1)
                    diagonals(g - 1, 1 - b, range(TOPK // 2, TOPK))
                    gelu(g, b)

                for hp in range(2 * HEADS):
                    wait_group(act, ("q", l, hp))
                    if hp >= 2:
                        wait_group(act, ("sc", l, hp - 2))
                    freed(nc.scalar.activation(qT[:, hp % 2, 0:T * P], at(("q", l, hp))[:, 0:T * P], ACT.Copy))
                    if hp == 3:
                        wait_taken(act, ("sc", l, 1))
                        if l > 0:
                            act.wait_ge(idx_ready, base - 1)
                        nc.scalar.activation(head_sc[:, 0, :, :].rearrange("p a k -> p (a k)"),
                                             scores[:, 0:256], ACT.Copy).then_inc(sc_in, 1)
                    if hp == 5:
                        gate_exps(0)
                wait_taken(act, ("sc", l, 2 * HEADS - 1))
                if l > 0:
                    act.wait_ge(idx_ready, base)
                nc.scalar.activation(head_sc[:, 1, :, :].rearrange("p a k -> p (a k)"),
                                     scores[:, 256:512], ACT.Copy).then_inc(sc_in, 1)
                gate_exps(1)
                gelu(0, 0)
                step(1, 1, first=True)
                with act.Fori(1, NH // 2 - 1) as i:
                    step(i * 2, 0)
                    step(i * 2 + 1, 1)
                step(NH - 2, 0)
                step(NH - 1, 1, last=True)
                diagonals(NH - 1, 1, range(TOPK))
            act.wait_ge(peer_done, LAYERS)
            for t in range(2):
                ins = nc.scalar.activation(junk, x_res[:, t, :], ACT.Square, accum_out=ss[:, t:t + 1])
                if t == 0:
                    chain(ins)
            ins.then_inc(sq_ready, 1)

        @block.gpsimd
        def _(pool):
            nc.gpsimd.memset(mhalf[:, :], -0.5).then_inc(pool_c, 1)
            pool.wait_ge(pool_c, 1)

            norms = [0]

            def power(dst, src, count):
                norms[0] += 1
                pool.wait_ge(ms_ready, norms[0])
                nc.gpsimd.tensor_tensor(dst, src, mhalf[:, 0:count], ALU.pow).then_inc(rstd_ready, 1)

            for l in range(LAYERS):
                T = q_tiles(l)
                power(rstd[:, :], ms[:, :], 4)
                pool.wait_ge(convw_in, 64 * (l + 1))
                pool.wait_ge(u_back, 32 * sum(q_tiles(k) for k in range(l + 1)))
                for buf, j in ((u_prev, 0), (u_next, 2)):
                    for t in range(T):
                        nc.gpsimd.tensor_tensor(buf[:, t, :], buf[:, t, :], conv_w[:, j, :], ALU.mult) \
                            .then_inc(uprev_ready, 1)
                for t in range(T):
                    power(da_r[:, t, :], da_ms[:, t, :], DA_HEADS)
                for t in range(T):
                    power(rstd[:, t:t + 1], ms[:, t:t + 1], 1)
                base = HEADS_BEFORE[l]
                NH = HEADS * T
                wait_group(pool, ("sc", l, 2 * HEADS - 1))

                def gather_u(g, b, j, first=False):
                    if not (first and j < U_SLOTS):
                        pool.wait_ge(dot_done, (g + base) * TOPK + j - U_SLOTS + 1)
                    stand_alone(pool)
                    pool.indirect_dma_start(u_rows[j % U_SLOTS], None, A["peer_u"],
                                            bass.IndirectOffsetOnAxis(idx_u[b][:, j:j + 1], 0)) \
                        .then_inc(u_in[j % U_SLOTS], 16)

                def gather_v(g, b, j, first=False):
                    if not (first and j < V_SLOTS):
                        pool.wait_ge(v_used, (g + base) * TOPK + j - V_SLOTS + 1)
                    stand_alone(pool)
                    pool.indirect_dma_start(v_rows[j % V_SLOTS], None, A["peer_v"],
                                            bass.IndirectOffsetOnAxis(idx_v[b][:, j:j + 1], 0)) \
                        .then_inc(v_in[j % V_SLOTS], 16)

                def step(g, b, first=False):
                    pool.wait_ge(idx_ready, g + (base + 1))
                    pool.wait_ge(idxv_ready, g + base)
                    for j in range(TOPK):
                        gather_u(g, b, j)
                        gather_v(g - 1, 1 - b, j, first)

                pool.wait_ge(idx_ready, base + 1)
                for j in range(TOPK):
                    gather_u(0, 0, j, True)
                step(1, 1, True)
                with pool.Fori(1, NH // 2) as i:
                    step(i * 2, 0)
                    step(i * 2 + 1, 1)
                pool.wait_ge(idxv_ready, base + NH)
                for j in range(TOPK):
                    gather_v(NH - 1, 1, j)
            power(rstd[:, 0:2], ms[:, 0:2], 2)

        @block.vector
        def _(dve):
            V = nc.vector
            counts = {}

            def done(ins, signal=dve_c):
                counts[signal.name] = counts.get(signal.name, 0) + 1
                ins.then_inc(signal, 1)
                dve.wait_ge(signal, counts[signal.name])

            def freed(ins):
                done(ins, dve_freed)

            dve.wait_ge(consts_in, CONSTS)
            dve.wait_ge(c_exp, 1)
            done(V.tensor_scalar(c_tmp[:, :], c_tmp[:, :], 1.0, None, ALU.add))
            done(V.reciprocal(c_tmp[:, :], c_tmp[:, :]))
            done(V.tensor_tensor(c_act[:, :, :].rearrange("p k s -> p (k s)"), c_raw[:, :], c_tmp[:, :], ALU.mult),
                 c_ready)
            for n in range(2):
                done(V.tensor_tensor(lam_p[:, n, :], lam_v[:, 2 * n, :], lam_v[:, 2 * n + 1, :], ALU.mult))
            done(V.tensor_reduce(lam_s[:, :, :].rearrange("p a l -> p (a l)"),
                                 lam_p[:, :, :].rearrange("p a (l d) -> p (a l) d", l=LAYERS), AX, ALU.add), lam_sum)
            dve.wait_ge(lam_exp, 1)
            done(V.tensor_tensor(lam_n[:, :], lam_s[:, 1, :], lam_s[:, 0, :], ALU.subtract))
            for l in range(LAYERS):
                done(V.tensor_scalar(lam_n[:, l:l + 1], lam_n[:, l:l + 1], -lam_init_of(l), None, ALU.add))
                done(V.tensor_scalar(dag[:, l, :], dag[:, l, :], 1.0 - lam_init_of(l), None, ALU.mult))
            done(V.tensor_scalar(nsinks[:, :, :], sinks[:, :, :], -1.0, None, ALU.mult))
            sq_count = 0
            rstd_count = 0
            o_count = 0

            def mean_square(tiles):
                nonlocal sq_count
                sq_count += 1
                dve.wait_ge(sq_ready, sq_count)
                done(V.tensor_scalar(ms[:, tiles], ss[:, tiles], 1.0 / D, EPS, ALU.mult, ALU.add), ms_ready)

            def await_power():
                nonlocal rstd_count
                rstd_count += 1
                dve.wait_ge(rstd_ready, rstd_count)

            for l in range(LAYERS):
                T, S = q_tiles(l), streams(l)
                dve.wait_ge(w3_in, 32 * (l + 1))
                done(V.scalar_tensor_tensor(f_dec, f_dec, -1.0, f_dec, ALU.mult, ALU.max), win_arg)

                def sine_argument(n):
                    key = ("flt1", l) if n == 0 else ("flt2", l)
                    wait_group(dve, key)
                    if n:
                        dve.wait_ge(sin_done, 2 * l + 1)
                    freed(V.tensor_scalar(f_arg, at(key)[0:FW, 0:256], fcol[:, l, 1 + n:2 + n], fcol[:, l, 0:1],
                                          ALU.add, ALU.mult))
                    done(V.tensor_scalar(f_rnd, f_arg, 1.0 / (2.0 * math.pi), ROUND, ALU.mult, ALU.add))
                    done(V.tensor_scalar(f_rnd, f_rnd, -ROUND, None, ALU.add))
                    done(V.scalar_tensor_tensor(f_arg, f_rnd, -C1, f_arg, ALU.mult, ALU.add))
                    done(V.scalar_tensor_tensor(f_arg, f_rnd, -C2, f_arg, ALU.mult, ALU.add))
                    done(V.tensor_scalar(f_arg, f_arg, PI_IN, -PI_IN, ALU.min, ALU.max), sin_arg)

                def windowed_filters():
                    for tt in range(2):
                        dve.wait_ge(win_done, 2 * l + tt + 1)
                        for o in range(2):
                            key = ("flt3", l, tt, o)
                            wait_group(dve, key)
                            freed(V.tensor_tensor(f_hw, at(key)[:, :], f_win[:, o * 512:(o + 1) * 512], ALU.mult))
                            c = slice(o * HYW, (o + 1) * HYW)
                            done(V.tensor_scalar(f_hw[:, HYW:512], f_hw[:, HYW:512], cols[:, 2 + tt:3 + tt], None,
                                                 ALU.mult))
                            done(V.tensor_tensor(f_sum[:, tt, c], f_hw[:, 0:HYW], f_hw[:, HYW:512], ALU.add))
                            done(V.tensor_tensor(f_dif[:, tt, c], f_hw[:, 0:HYW], f_hw[:, HYW:512], ALU.subtract),
                                 fsum_ready)

                sine_argument(0)
                dve.wait_ge(bmod_in, 32 * (l + 1))
                for n in range(16):
                    key = ("mod", l, n)
                    c = slice(n * 384, (n + 1) * 384)
                    wait_group(dve, key)
                    freed(V.tensor_tensor(mod_rows[:, c], at(key)[0:2, 0:384], bmod_rows[:, c], ALU.add))
                    if n == 1:
                        sine_argument(1)
                    if n == 3:
                        windowed_filters()
                    if n == 8:
                        mean_square(slice(0, 4))
                        await_power()
                        for t in range(4):
                            done(V.tensor_scalar(area_y[:, t, :], x_res[:, t, :], rstd[:, t:t + 1], None, ALU.mult),
                                 xn_ready)
                a2_row = mod_rows[:, 4 * D:5 * D]
                done(V.scalar_tensor_tensor(a2_row, a2_row, 1.0, g2_rows, ALU.add, ALU.mult), rows_ready)
                wait_group(dve, ("col", l))
                freed(V.tensor_copy(modc[:, :, :].rearrange("p k s -> p (k s)"), at(("col", l))[:, 0:4 * KD]))
                done(V.scalar_tensor_tensor(a1[:, :, :], modc[:, KD:2 * KD, :], 1.0,
                                            g1[:, l, :].unsqueeze(2).to_broadcast([P, KD, 2]), ALU.add, ALU.mult),
                     mod_ready)
                for kk in range(0, KD, 2):
                    wait_group(dve, ("hT", l, kk))
                    for s in range(2):
                        ins = V.tensor_scalar(hT[:, kk, s * 256:(s + 1) * 256],
                                              at(("hT", l, kk))[:, s * 256:(s + 1) * 256],
                                              a1[:, kk, s:s + 1], modc[:, kk, s:s + 1], ALU.mult, ALU.add)
                        (freed if s else done)(ins)

                def conv():
                    dve.wait_ge(convw_in, 64 * (l + 1))
                    for t in range(T):
                        for c in range(2):
                            wait_taken(dve, ("pj", l, c, t))
                    dve.wait_ge(u_back, 32 * sum(q_tiles(k) for k in range(l + 1)))
                    hy = proj[:, 0:T, 0:HY_COLS]

                    def tap(j):
                        return conv_w[:, j:j + 1, :].to_broadcast([P, T, HY_COLS])
                    done(V.tensor_tensor(hy, hy, tap(1), ALU.mult))
                    done(V.tensor_tensor(hy, hy, tap(3), ALU.add))
                    dve.wait_ge(uprev_ready, 2 * sum(q_tiles(k) for k in range(l + 1)))
                    done(V.tensor_tensor(hy, hy, u_prev[:, 0:T, :], ALU.add))
                    done(V.tensor_tensor(hy, hy, u_next[:, 0:T, :], ALU.add), conv_done)

                def rotate(first_col, heads, dim, r0, chunks):
                    m = dim // 4
                    for t in range(2):
                        for c in chunks:
                            wait_taken(dve, ("pj", l, c, t))
                        xc = proj[:, t, first_col:first_col + heads * dim]
                        xv = xc.rearrange("p (h d) -> p h d", d=dim)
                        x4 = xc.rearrange("p (h a b m) -> p h a b m", a=2, b=2, m=m)
                        t1 = rope_1[:, 0:heads * dim].rearrange("p (h d) -> p h d", d=dim)
                        t2 = rope_2[:, 0:heads * dim].rearrange("p (h d) -> p h d", d=dim)
                        t4 = rope_2[:, 0:heads * dim].rearrange("p (h a b m) -> p h a b m", a=2, b=2, m=m)
                        cos = rope[:, t, r0:r0 + dim].unsqueeze(1).to_broadcast([P, heads, dim])
                        sin = rope[:, t, r0 + dim:r0 + 2 * dim].rearrange("p (a b m) -> p a b m", a=2, b=2)
                        done(V.tensor_tensor(t1, xv, cos, ALU.mult))
                        for half in range(2):
                            done(V.tensor_tensor(t4[:, :, :, half, :], x4[:, :, :, 1 - half, :],
                                                 sin[:, :, half, :].unsqueeze(1).to_broadcast([P, heads, 2, m]),
                                                 ALU.mult))
                        done(V.tensor_tensor(xv, t1, t2, ALU.add), roped)

                for c, t in proj_units(l):
                    if t % 2 == 0:
                        wait_group(dve, ("pj", l, c, t))
                        freed(V.tensor_copy(proj[:, t, c * 384:(c + 1) * 384], at(("pj", l, c, t))[:, 0:384]))
                    if (c, t) == (4, 0):
                        rotate(WA0, 10, 64, 0, (2, 3))
                    if (c, t) == (5, 0):
                        conv()
                rotate(DA0, 16, 32, 128, (4, 5))
                dve.wait_ge(hybias_in, 16 * (l + 1))
                for k in range(5):
                    wait_taken(dve, ("spec", l, k))
                W = S * HYW

                def sv(ap):
                    return ap[:, 0:W].rearrange("p (s c) -> p s c", c=HYW)

                for o in range(2):
                    for m in range(2):
                        re, im = at(("re", l, o, m)), at(("im", l, o, m))
                        h = [spec[:, k, o * HYW:(o + 1) * HYW].unsqueeze(1).to_broadcast([P, S, HYW])
                             for k in (m, 2 + m, 4 if m == 0 else 1)]
                        wait_group(dve, ("im", l, o, m))
                        done(V.tensor_tensor(sv(yre[:, m, :]), sv(re), h[0], ALU.mult))
                        done(V.tensor_tensor(sv(hy_tmp), sv(im), h[1], ALU.mult))
                        done(V.tensor_tensor(yre[:, m, 0:W], yre[:, m, 0:W], hy_tmp[:, 0:W], ALU.subtract))
                        freed(V.tensor_tensor(sv(yim[:, m, :]), sv(re), h[1], ALU.mult))
                        freed(V.tensor_tensor(sv(hy_tmp), sv(im), h[2], ALU.mult))
                        done(V.tensor_tensor(yim[:, m, 0:W], yim[:, m, 0:W], hy_tmp[:, 0:W], ALU.add), y_spec)
                    for tt in range(2):
                        key = ("inv", l, o, tt)
                        pj = area_p[:, :].rearrange("p (s t c) -> p s t c", s=2, t=2)
                        z = pj[:, 0:S, tt, 512:768] if o == 0 else z_buf[:, tt, 0:S, :]
                        wait_group(dve, key)
                        done(V.tensor_tensor(sv(hy_tmp), z, hy_bias[:, o:o + 1, :].to_broadcast([P, S, HYW]),
                                             ALU.mult))
                        freed(V.tensor_tensor(hy_tmp[:, 0:W], hy_tmp[:, 0:W], at(key)[:, 0:W], ALU.add))
                        dst = z_buf[:, tt, 0:S, :] if o == 0 else \
                            area_y[:, :, :].rearrange("p (s t) c -> p s t c", s=2)[:, 0:S, tt, 0:HYW]
                        done(V.tensor_tensor(dst, sv(hy_tmp), pj[:, 0:S, tt, o * HYW:(o + 1) * HYW], ALU.mult),
                             z_ready if o == 0 else dve_c)
                maps = attention_maps(l)
                maps_before = sum(len(attention_maps(k)) for k in range(l))

                def stats(n):
                    kind, t, h, m = maps[n]
                    c = stat_column(*maps[n])
                    key = ("s", l, n)
                    wait_group(dve, key)
                    width = 512 if t < 2 else 256
                    if kind == "wa" and t < 2:
                        freed(V.tensor_tensor_reduce(out=p_buf[:, n % (AHEAD + 1), :], in0=at(key)[:, :], in1=mask[:, t, :],
                                                     scale=1.0, scalar=LOW, op0=ALU.add, op1=ALU.max,
                                                     accum_out=mx[:, c:c + 1]))
                    else:
                        done(V.tensor_reduce(mx[:, c:c + 1], at(key)[:, 0:width], AX, ALU.max))
                    if kind == "wa":
                        done(V.tensor_scalar(nm[:, c:c + 1], mx[:, c:c + 1], -WA_SCALE, nsinks[:, l, h:h + 1],
                                             ALU.mult, ALU.min), neg_max)
                    else:
                        done(V.tensor_scalar(nm[:, c:c + 1], mx[:, c:c + 1], -DA_SCALE, None, ALU.mult), neg_max)

                def combine(n):
                    kind, t, h, m = maps[n]
                    c = stat_column(*maps[n])
                    width = 512 if t < 2 else 256
                    dve.wait_ge(exp_done, maps_before + n + 1)
                    done(V.reciprocal(rr[:, 0:1], lsum[:, c:c + 1]))
                    done(V.scalar_tensor_tensor(rr[:, 1:2], rr[:, 0:1], lam_n[:, l:l + 1], lsum[:, c - 1:c],
                                                ALU.mult, ALU.mult))
                    p0, p1 = p_buf[:, (n - 1) % (AHEAD + 1), 0:width], p_buf[:, n % (AHEAD + 1), 0:width]
                    done(V.scalar_tensor_tensor(p1, p1, rr[:, 1:2], p0, ALU.mult, ALU.add), comb_done)

                def take_outputs(n):
                    nonlocal o_count
                    kind, t, h, m = maps[n]
                    o_count += 1
                    dve.wait_ge(pv_done, o_count)
                    width, c = (512, 256) if kind == "wa" else (256, 768)
                    done(V.tensor_copy(area_y[:, t, c:c + width], bank[BANKS + (o_count - 1) % 2][:, 0:width]), o_taken)

                tiles_before = sum(q_tiles(k) for k in range(l))

                def sink_scores(t):
                    done(V.tensor_tensor(esink[:, t, :], nm[:, t * WA_HEADS:(t + 1) * WA_HEADS], sinks[:, l, :],
                                         ALU.add), sink_arg)

                def finish_tile(t):
                    da = area_y[:, t, 768:1024]
                    dh = da.rearrange("p (h d) -> p h d", d=64)
                    c = 32 + t * 2 * DA_HEADS
                    done(V.reciprocal(da_r0[:, :], lsum[:, c:c + 2 * DA_HEADS]))
                    r0 = da_r0[:, :].rearrange("p (h m) -> p h m", m=2)[:, :, 0:1]
                    done(V.tensor_tensor(dh, dh, r0.to_broadcast([P, DA_HEADS, 64]), ALU.mult))
                    done(V.tensor_tensor(da_sq[:, t, :], da, da, ALU.mult))
                    done(V.tensor_reduce(da_ss[:, t, :], da_sq[:, t, :].rearrange("p (h d) -> p h d", d=64), AX,
                                         ALU.add))
                    done(V.tensor_scalar(da_ms[:, t, :], da_ss[:, t, :], 1.0 / 64, EPS, ALU.mult, ALU.add), ms_ready)
                    dve.wait_ge(sink_exp, tiles_before + t + 1)
                    done(V.tensor_tensor(esum[:, t, :], esink[:, t, :], lsum[:, t * WA_HEADS:(t + 1) * WA_HEADS],
                                         ALU.add))
                    done(V.reciprocal(esum[:, t, :], esum[:, t, :]))
                    wa = area_y[:, t, 256:768].rearrange("p (h d) -> p h d", d=64)
                    done(V.tensor_tensor(wa, wa, esum[:, t, :].unsqueeze(2).to_broadcast([P, WA_HEADS, 64]), ALU.mult))
                    await_power()
                    done(V.tensor_tensor(dh, dh, da_r[:, t, :].unsqueeze(2).to_broadcast([P, DA_HEADS, 64]), ALU.mult))
                    done(V.tensor_tensor(dh, dh, dag[:, l:l + 1, :].to_broadcast([P, DA_HEADS, 64]), ALU.mult),
                         y_ready)

                for n in range(AHEAD):
                    stats(n)
                finished = None
                e = 0
                for n, unit in enumerate(maps):
                    if unit[0] == "da" and has_pv(unit):
                        combine(n)
                    if n + AHEAD < len(maps):
                        stats(n + AHEAD)
                    if has_pv(unit):
                        if GROUPS[GROUP_AT["pt", l, n]][1] == "dve":
                            wait_group(dve, ("pt", l, n))
                            width = 512 if unit[1] < 2 else 256
                            freed(V.tensor_copy(pT_buf[:, e % 2, 0:width], at(("pt", l, n))[:, 0:width]))
                        e += 1
                        if finished is not None:
                            take_outputs(finished)
                            if maps[finished][0] == "wa":
                                sink_scores(maps[finished][1])
                            else:
                                finish_tile(maps[finished][1])
                            finished = None
                        if unit[2] == (WA_HEADS if unit[0] == "wa" else DA_HEADS) - 1:
                            finished = n
                take_outputs(finished)
                finish_tile(T - 1)
                for kk in range(0, KD, 2):
                    wait_group(dve, ("yT", l, kk))
                    freed(V.tensor_copy(hT[:, kk, 0:T * P], at(("yT", l, kk))[:, 0:T * P]))
                dve.wait_ge(rows_in, 48 * sum(streams(k) for k in range(l + 1)))

                def modulated_norm(t):
                    await_power()
                    done(V.scalar_tensor_tensor(area_y[:, t, :], x_res[:, t, :], rstd[:, t:t + 1],
                                                a2_bc[:, t // 2, :], ALU.mult, ALU.mult))
                    done(V.tensor_tensor(area_y[:, t, :], area_y[:, t, :], b2_bc[:, t // 2, :], ALU.add), h2_ready)

                for t in range(T):
                    for n in range(4):
                        key = ("wo", l, n, t)
                        c = slice(n * 256, (n + 1) * 256)
                        wait_group(dve, key)
                        freed(V.tensor_tensor(res_tmp, at(key)[:, 0:256], gate_bc[:, t // 2, c], ALU.mult))
                        done(V.tensor_tensor(x_res[:, t, c], x_res[:, t, c], res_tmp, ALU.add),
                             x_done if n == 3 else dve_c)
                    mean_square(slice(t, t + 1))
                    modulated_norm(t)
                base = HEADS_BEFORE[l]
                NH = HEADS * T
                CH = 27
                PART_FIRST = [0, 5, 10, 15, 20, 23, CH]
                chain0 = counts.get(dve_c.name, 0)

                def top_k(g, b, part):
                    k = [PART_FIRST[part]]

                    def link(ins):
                        k[0] += 1
                        ins.then_inc(dve_c, 1)
                        dve.wait_ge(dve_c, g * CH + (chain0 + k[0]))
                        if k[0] in (1, 2, 3, 4, 5, 6, 7, 8, 9, 12, 13, 14, 15, 16):
                            stand_alone(dve)

                    c3 = cand.rearrange("p (a b) -> p a b", a=TOPK)
                    oh = onehot.rearrange("p (s r) -> p s r", s=TOPK)
                    if part == 0:
                        dve.wait_ge(sc_in, g + (base + 1))
                    if part in (0, 1, 3):
                        stand_alone(dve)
                    if part in (0, 1):
                        a, src = part, head_sc[:, b, part, :]
                        link(V.max(top_s[:, a, 0:8], src))
                        link(V.max_index(top_i[:, a, 0:8], top_s[:, a, 0:8], src))
                        link(V.match_replace(sc_left[:, a, :], top_s[:, a, 0:8], src, LOW))
                        link(V.max(top_s[:, a, 8:16], sc_left[:, a, :]))
                        link(V.max_index(top_i[:, a, 8:16], top_s[:, a, 8:16], sc_left[:, a, :]))
                    if part == 2:
                        link(V.tensor_copy(top_f[:, :, :], top_i[:, :, :]))
                        link(V.tensor_tensor(c3, top_s[:, 0, :].unsqueeze(2).to_broadcast([P, TOPK, TOPK]),
                                             top_s[:, 1, :].unsqueeze(1).to_broadcast([P, TOPK, TOPK]), ALU.add))
                        link(V.max(best_s[:, 0:8], cand))
                        link(V.match_replace(cand2, best_s[:, 0:8], cand, LOW))
                        link(V.max(best_s[:, 8:16], cand2))
                        V.tensor_scalar(nbest[:, :], best_s[:, 0:1], -1.0, None, ALU.mult).then_inc(best_ready, 1)
                    if part == 3:
                        link(V.max_index(best_j[:, 0:8], best_s[:, 0:8], cand))
                        link(V.max_index(best_j[:, 8:16], best_s[:, 8:16], cand2))
                        link(V.tensor_scalar(part_u[:, 0, :], best_j[:, :], 4, None, ALU.logical_shift_right))
                        link(V.tensor_scalar(part_u[:, 1, :], best_j[:, :], 15, None, ALU.bitwise_and))
                        link(V.tensor_copy(part_f[:, :, :], part_u[:, :, :]))
                    if part in (4, 5):
                        a = part - 4
                        link(V.tensor_tensor(oh, part_f[:, a, :].unsqueeze(2).to_broadcast([P, TOPK, TOPK]),
                                             iota16[:, :].unsqueeze(1).to_broadcast([P, TOPK, TOPK]), ALU.is_equal))
                        link(V.tensor_tensor(oh, oh, top_f[:, a, :].unsqueeze(1).to_broadcast([P, TOPK, TOPK]),
                                             ALU.mult))
                        link(V.tensor_reduce(pick[:, a, :], oh, AX, ALU.add))
                    if part == 5:
                        link(V.tensor_scalar(pick[:, 0, :], pick[:, 0, :], float(NKEYS), float(l * NEXP),
                                             ALU.mult, ALU.add))
                        V.tensor_tensor(idx_u[b][:, :], pick[:, 0, :], pick[:, 1, :], ALU.add).then_inc(idx_ready, 1)
                        dve.wait_ge(gate_exp, g + (base + 1))
                        V.reciprocal(rbest[:, :], esumb[:, :]).then_inc(gate_r, 1)
                        dve.wait_ge(gate_r, g + (base + 1))
                        V.tensor_scalar(gate[:, b, :], ebest[:, :], rbest[:, 0:1], None, ALU.mult) \
                            .then_inc(gate_done, 1)
                    assert k[0] == PART_FIRST[part + 1]

                def weights_of(g, b):
                    dve.wait_ge(gelu_done, g + (base + 1))
                    dve.wait_ge(gate_done, g + (base + 1))
                    V.tensor_tensor(wgt[:, b, :], gel[:, b, :], gate[:, b, :], ALU.mult).then_inc(w_ready, 1)

                def accumulate(g, b):
                    dve.wait_ge(v_used, (g + base) * TOPK + TOPK)
                    tile = g // HEADS
                    for half in range(2):
                        dst = area_a[:, bass.ds(tile * D + half * 512, 512)]
                        ins = V.tensor_tensor(dst, dst, bank[2 * b + half][:, :], ALU.add)
                        ins.then_inc(acc_done, 1)
                    dve.wait_ge(acc_done, (g + (base + 1)) * 2)

                def dot(g, b, j):
                    dve.wait_ge(u_in[j % U_SLOTS], (g + base) * (16 * TOPK // U_SLOTS) + 16 * (j // U_SLOTS) + 16)
                    tile = g // HEADS
                    V.scalar_tensor_tensor(out=dot_junk, in0=u_rows[j % U_SLOTS], scalar=1.0,
                                           in1=y_flat[:, bass.ds(tile * D, D)], op0=ALU.mult, op1=ALU.mult,
                                           accum_out=dots[:, b, j:j + 1]).then_inc(dot_done, 1)
                    dve.wait_ge(dot_done, (g + base) * TOPK + j + 1)

                def step(g, b, first=False, second=False, last=False):
                    if not first:
                        weights_of(g - 1, 1 - b)
                    for j in range(TOPK):
                        dot(g, b, j)
                        if j == 1:
                            if not first and not second:
                                accumulate(g - 2, b)
                            dve.wait_ge(idx_ready, g + (base + 1))
                            V.tensor_copy(idx_v[b][:, :], idx_u[b][:, :]).then_inc(idxv_ready, 1)
                        if j % 2 == 0 and j // 2 < 6 and not last:
                            top_k(g + 1, 1 - b, j // 2)

                sc4 = scores.rearrange("p (t h k) -> p t h k", t=4, h=16)
                for hp in range(2 * HEADS):
                    wait_group(dve, ("sc", l, hp))
                    freed(V.tensor_copy(sc4[:, 0:T, hp, :],
                                        at(("sc", l, hp))[:, 0:T * P].rearrange("p (t k) -> p t k", k=P)))
                    if hp == 3:
                        for part in range(6):
                            top_k(0, 0, part)
                V.memset(o_acc[:, 0:T, :], 0.0).then_inc(acc_zero, 1)
                dve.wait_ge(acc_zero, l + 1)
                step(0, 0, first=True)
                step(1, 1, second=True)
                with dve.Fori(1, NH // 2 - 1) as i:
                    step(i * 2, 0)
                    step(i * 2 + 1, 1)
                step(NH - 2, 0)
                step(NH - 1, 1, last=True)
                weights_of(NH - 1, 1)
                accumulate(NH - 2, 0)
                accumulate(NH - 1, 1)
                counts[dve_c.name] = chain0 + NH * CH
                dve.wait_ge(gate5_in, 16 * sum(streams(k) for k in range(l + 1)))
                for t in range(T):
                    done(V.tensor_tensor(o_acc[:, t, :], o_acc[:, t, :], gate_bc[:, t // 2, :], ALU.mult))
                    done(V.tensor_tensor(x_res[:, t, :], x_res[:, t, :], o_acc[:, t, :], ALU.add),
                         peer_done if t == T - 1 else dve_c)
            mean_square(slice(0, 2))
            await_power()
            dve.wait_ge(fg_in, 16)
            for t in range(2):
                done(V.scalar_tensor_tensor(area_y[:, t, :], x_res[:, t, :], rstd[:, t:t + 1], final_g,
                                            ALU.mult, ALU.mult), out_ready)


def _tables():
    n = 2 * SEQ
    t = np.arange(SEQ)
    ang = 2.0 * np.pi * ((t[:, None] * t[None, :]) % n) / n
    cos, sin = np.cos(ang), -np.sin(ang)
    sin[:, 0] = 0.0
    alt = np.where(t % 2 == 0, 1.0, -1.0)
    cos_alt, sin_alt = cos.copy(), sin.copy()
    cos_alt[:, 0] = alt
    sin_alt[:, 0] = alt

    def tiles(a):
        return a.reshape(2, P, -1).transpose(1, 0, 2)

    f = np.float32
    tl = np.linspace(0.0, 1.0, SEQ, dtype=f)
    bands = np.linspace(1e-4, 15, 16, dtype=f)
    phase = (f(2.0 * math.pi / SEQ) * np.arange(SEQ, dtype=f)[:, None] * bands).astype(f)
    feat = np.concatenate([tl[:, None], np.cos(phase), -np.sin(phase)], axis=-1).astype(f)
    cols = np.zeros((P, 6), f)
    cols[:, 0:2] = -tl.reshape(2, P).T
    cols[:, 2:4] = 1.0
    cols[0, 2] = 0.0
    cols[:, 4:6] = 2.0 / n
    cols[0, 4] = 1.0 / n
    row, col = (t // GRID_W).astype(f), (t % GRID_W).astype(f)
    parts = []
    for dim in (64, 32):
        axis_dim = dim // 2
        inv = (f(10000.0) ** (-np.arange(0, axis_dim, 2, dtype=f) / f(axis_dim))).astype(f)
        angs = np.stack([row[:, None] * inv, col[:, None] * inv], axis=1)
        c, s = np.cos(angs), np.sin(angs)
        parts.append(np.stack([c, c], axis=2).reshape(SEQ, dim))
        parts.append(np.stack([-s, s], axis=2).reshape(SEQ, dim))
    mask = np.zeros((SEQ, 512), f)
    mask[:, 0:SEQ] = np.where(np.abs(t[:, None] - t[None, :]) <= 128, 0.0, -1e30)
    return {
        "k_ident": np.eye(P), "k_dft_c": tiles(cos), "k_dft_s": tiles(sin_alt), "k_dft_i": tiles(sin_alt.T),
        "k_dft_cn": tiles(cos_alt[:, 0:P]), "k_dft_s0": tiles(sin[:, 0:P]), "k_cols": cols, "k_feat": feat.T,
        "k_rope": tiles(np.concatenate(parts, axis=1)), "k_mask": tiles(mask),
        "k_iota": np.broadcast_to(np.arange(TOPK), (P, TOPK)), "k_zrows": np.zeros((LAYERS, 2, 2, HY_COLS)),
    }


def _lay_out(i):
    L = LAYERS

    def by_part(a):
        a = a.reshape(a.shape[:-1] + (-1, P))
        return np.moveaxis(a, -1, 0)

    same = ["x", "ctx", "w_mod", "hy_conv_w", "hy_conv_b", "hy_w3", "hy_bias", "wa_sink", "da_lq1",
            "da_lk1", "da_lq2", "da_lk2", "da_norm_g", "w_out", "peer_wq",
            "final_g", "b_mod", "norm2_g"]
    out = {n: i[n] for n in same}
    out["c_cols"] = np.moveaxis(by_part(np.stack([i["c"][0], i["c_ctx"]])), 1, 2).reshape(P, KD * 2)
    w = i["w_in"].copy()
    q = i["w_in"][:, :, WA0:WA0 + 512].reshape(L, D, WA_KV, 4, 64)
    w[:, :, WA0:WA0 + 512] = q.transpose(0, 1, 3, 2, 4).reshape(L, D, 512)
    out["w_in"] = w
    out["g1"] = by_part(i["norm1_g"])
    out["fcol"] = np.stack([i["hy_freq"], i["hy_b1"], i["hy_b2"]]).transpose(2, 1, 0)
    out["hy_w1"] = i["hy_w1"].transpose(1, 0, 2)
    out["hy_w2"] = i["hy_w2"].transpose(1, 0, 2)
    out["hy_decay"] = i["hy_decay"].reshape(L, -1)
    out["keysT"] = i["peer_keys"].transpose(0, 4, 1, 2, 3).reshape(L, P, 2 * HEADS, NKEYS)
    out["peer_u"] = i["peer_u"].reshape(L * NEXP, D)
    out["peer_v"] = i["peer_v"].reshape(L * NEXP, D)
    return out


def kernel(**inputs):
    import concourse.bacc as bacc
    from concourse.bass_utils import run_bass_kernel_spmd

    nc = bacc.Bacc("TRN2", target_bir_lowering=False, num_devices=1)
    arrays = {n: np.asarray(a) for n, a in inputs.items()}
    arrays = {n: np.ascontiguousarray(a) for n, a in _lay_out(arrays).items()}
    arrays.update({n: np.ascontiguousarray(a, dtype=np.float32) for n, a in _tables().items()})
    aps = {n: nc.dram_tensor(n, a.shape, F32, kind="ExternalInput").ap() for n, a in arrays.items()}
    out = nc.dram_tensor("out", (1, SEQ, D), F32, kind="ExternalOutput").ap()
    build(nc, aps, out)
    r = run_bass_kernel_spmd(nc, [arrays], core_ids=[0])
    return r.results[0]["out"]
```
